# Optimizing a Trainium2 kernel written in Bass

```python
import jax, jax.numpy as jnp
from jax import lax
import numpy as np
import math

D_MODEL = 2048
BATCH = 1
SEQ = 256
DEPTH = 1

N_MIXERS = 3
EPS = 1e-6
SB_HEADS = 16
SB_HEAD_DIM = D_MODEL // SB_HEADS
SB_WIDTH = SB_HEADS * SB_HEAD_DIM
Q_BLOCK = 128
GM_CHUNK = 128
GM_GROUPS = 16
GM_WIDTH = D_MODEL
GM_GROUP_DIM = GM_WIDTH // GM_GROUPS
SSD_INNER = 2 * D_MODEL
SSD_HEAD_DIM = 64
SSD_HEADS = SSD_INNER // SSD_HEAD_DIM
SSD_GROUPS = 8
SSD_HPG = SSD_HEADS // SSD_GROUPS
SSD_STATE = 128
SSD_CONV = 4
SSD_CHUNK = 128
SSD_CONV_DIM = SSD_INNER + 2 * SSD_GROUPS * SSD_STATE
SSD_PROJ = SSD_INNER + SSD_CONV_DIM + SSD_HEADS
MLP_HIDDEN = 4 * D_MODEL
N_A = len(range(0, DEPTH, N_MIXERS))
N_B = len(range(1, DEPTH, N_MIXERS))
N_C = len(range(2, DEPTH, N_MIXERS))


def rms_norm(x, g):
    xf = x.astype(jnp.float32)
    y = xf * lax.rsqrt(jnp.mean(xf * xf, axis=-1, keepdims=True) + EPS)
    return (y * g.astype(jnp.float32)).astype(x.dtype)

def stick_breaking_attention(h, w_qkv, q_g, k_g, w_o):
    b, s, _ = h.shape
    q, k, v = jnp.split(h @ w_qkv, 3, axis=-1)
    q = rms_norm(q.reshape(b, s, SB_HEADS, SB_HEAD_DIM), q_g).transpose(0, 2, 1, 3)
    k = rms_norm(k.reshape(b, s, SB_HEADS, SB_HEAD_DIM), k_g).transpose(0, 2, 1, 3)
    v = v.reshape(b, s, SB_HEADS, SB_HEAD_DIM).transpose(0, 2, 1, 3)
    scale = SB_HEAD_DIM ** -0.5
    n_blk = s // Q_BLOCK
    q_blocks = q.reshape(b, SB_HEADS, n_blk, Q_BLOCK, SB_HEAD_DIM).transpose(2, 0, 1, 3, 4)
    k_pos = jnp.arange(s)

    def one_block(args):
        qb, start = args
        z = jnp.einsum('bhqd,bhkd->bhqk', qb, k).astype(jnp.float32) * scale
        q_pos = start + jnp.arange(Q_BLOCK)
        mask = k_pos[None, :] < q_pos[:, None]
        log_beta = jax.nn.log_sigmoid(z)
        log_1m = jnp.where(mask, jax.nn.log_sigmoid(-z), 0.0)
        suffix = lax.cumsum(log_1m, axis=3, reverse=True) - log_1m
        a = jnp.where(mask, jnp.exp(log_beta + suffix), 0.0)
        return jnp.einsum('bhqk,bhkd->bhqd', a.astype(v.dtype), v)

    starts = jnp.arange(n_blk, dtype=jnp.int32) * Q_BLOCK
    o = lax.map(one_block, (q_blocks, starts))
    o = o.transpose(1, 0, 3, 2, 4).reshape(b, s, SB_WIDTH)
    return o @ w_o

def chunked_spatial_gating(h, w_in, v_g, w_s, b_s, w_o):
    b, s, _ = h.shape
    u, v = jnp.split(jax.nn.gelu(h @ w_in, approximate=False), 2, axis=-1)
    v = rms_norm(v, v_g)
    n_chunk = s // GM_CHUNK
    v = v.reshape(b, n_chunk, GM_CHUNK, GM_GROUPS, GM_GROUP_DIM)
    u = u.reshape(b, n_chunk, GM_CHUNK, GM_GROUPS, GM_GROUP_DIM)
    causal = jnp.tril(jnp.ones((GM_CHUNK, GM_CHUNK), dtype=bool))
    w = jnp.where(causal[None], w_s, 0.0)
    mixed = jnp.einsum('gts,bcsgd->bctgd', w.astype(v.dtype), v) + b_s.T[:, :, None]
    y = (u * mixed).reshape(b, s, GM_WIDTH)
    return y @ w_o

def ssd_chunked_scan(x, dt, a, bm, cm):
    b, s = x.shape[:2]
    c, L = s // SSD_CHUNK, SSD_CHUNK
    xs = (x * dt[..., None]).reshape(b, c, L, SSD_GROUPS, SSD_HPG, SSD_HEAD_DIM)
    da = (dt * a).reshape(b, c, L, SSD_GROUPS, SSD_HPG).transpose(0, 3, 4, 1, 2)
    bc = bm.reshape(b, c, L, SSD_GROUPS, SSD_STATE)
    cc = cm.reshape(b, c, L, SSD_GROUPS, SSD_STATE)
    a_cum = jnp.cumsum(da, axis=-1)
    seg = a_cum[..., :, None] - a_cum[..., None, :]
    tri = jnp.tril(jnp.ones((L, L), dtype=bool))
    decay = jnp.exp(jnp.where(tri, seg, -jnp.inf))
    cb = jnp.einsum('bclgn,bcsgn->bgcls', cc, bc)
    y_diag = jnp.einsum('bgcls,bgrcls,bcsgrp->bclgrp', cb, decay, xs)
    decay_states = jnp.exp(a_cum[..., -1:] - a_cum)
    states = jnp.einsum('bclgn,bgrcl,bclgrp->cbgrpn', bc, decay_states, xs)
    chunk_decay = jnp.exp(a_cum[..., -1]).transpose(3, 0, 1, 2)

    def step(carry, inp):
        st, dec = inp
        return carry * dec[..., None, None] + st, carry

    _, prev = lax.scan(step, jnp.zeros_like(states[0]), (states, chunk_decay))
    y_off = jnp.einsum('bclgn,cbgrpn,bgrcl->bclgrp', cc, prev, jnp.exp(a_cum))
    return (y_diag + y_off).reshape(b, s, SSD_GROUPS, SSD_HPG, SSD_HEAD_DIM)

def ssd_mixer(h, w_in, conv_w, conv_b, dt_bias, a_log, d_skip, norm_g, w_o):
    b, s, _ = h.shape
    z, xbc, dt = jnp.split(h @ w_in, [SSD_INNER, SSD_INNER + SSD_CONV_DIM], axis=-1)
    xbc = lax.conv_general_dilated(xbc, conv_w[:, None, :].astype(xbc.dtype), window_strides=(1,),
                                   padding=[(SSD_CONV - 1, 0)],
                                   dimension_numbers=('NWC', 'WIO', 'NWC'),
                                   feature_group_count=SSD_CONV_DIM) + conv_b
    xbc = jax.nn.silu(xbc)
    xi, bm, cm = jnp.split(xbc, [SSD_INNER, SSD_INNER + SSD_GROUPS * SSD_STATE], axis=-1)
    f32 = jnp.float32
    dt = jax.nn.softplus(dt.astype(f32) + dt_bias.astype(f32))
    a = -jnp.exp(a_log.astype(f32))
    xi = xi.astype(f32).reshape(b, s, SSD_GROUPS, SSD_HPG, SSD_HEAD_DIM)
    y = ssd_chunked_scan(xi, dt.reshape(b, s, SSD_GROUPS, SSD_HPG), a.reshape(SSD_GROUPS, SSD_HPG),
                         bm.astype(f32).reshape(b, s, SSD_GROUPS, SSD_STATE),
                         cm.astype(f32).reshape(b, s, SSD_GROUPS, SSD_STATE))
    y = y + d_skip.astype(f32).reshape(SSD_GROUPS, SSD_HPG)[:, :, None] * xi
    y = y.reshape(b, s, SSD_INNER).astype(h.dtype) * jax.nn.silu(z)
    y = rms_norm(y.reshape(b, s, SSD_GROUPS, SSD_INNER // SSD_GROUPS),
                 norm_g.reshape(SSD_GROUPS, SSD_INNER // SSD_GROUPS)).reshape(b, s, SSD_INNER)
    return y @ w_o

def squared_relu_mlp(h, w_in, w_out):
    return jnp.square(jax.nn.relu(h @ w_in)) @ w_out

def first_inputs(seed: int = 0) -> dict:
    key = jax.random.key(seed)
    ks = jax.random.split(key, 24)
    nrm = jax.random.normal
    f32 = jnp.float32
    d = D_MODEL
    dt = jnp.exp(jax.random.uniform(ks[14], (N_C, SSD_HEADS), f32, np.log(1e-3), np.log(1e-1)))
    return {
        "x": nrm(ks[0], (BATCH, SEQ, d), f32),
        "norm_mix_g": 1.0 + 0.02 * nrm(ks[1], (DEPTH, d), f32),
        "norm_mlp_g": 1.0 + 0.02 * nrm(ks[2], (DEPTH, d), f32),
        "sb_w_qkv": nrm(ks[3], (N_A, d, 3 * SB_WIDTH), f32) * d ** -0.5,
        "sb_q_norm_g": 1.0 + 0.02 * nrm(ks[4], (N_A, SB_HEAD_DIM), f32),
        "sb_k_norm_g": 1.0 + 0.02 * nrm(ks[5], (N_A, SB_HEAD_DIM), f32),
        "sb_w_o": nrm(ks[6], (N_A, SB_WIDTH, d), f32) * SB_WIDTH ** -0.5,
        "gm_w_in": nrm(ks[7], (N_B, d, 2 * GM_WIDTH), f32) * d ** -0.5,
        "gm_v_norm_g": 1.0 + 0.02 * nrm(ks[8], (N_B, GM_WIDTH), f32),
        "gm_w_s": nrm(ks[9], (N_B, GM_GROUPS, GM_CHUNK, GM_CHUNK), f32) * (1.0 / GM_CHUNK),
        "gm_b_s": 1.0 + 0.02 * nrm(ks[10], (N_B, GM_GROUPS, GM_CHUNK), f32),
        "gm_w_o": nrm(ks[11], (N_B, GM_WIDTH, d), f32) * GM_WIDTH ** -0.5,
        "ssd_w_in": nrm(ks[12], (N_C, d, SSD_PROJ), f32) * d ** -0.5,
        "ssd_conv_w": nrm(ks[13], (N_C, SSD_CONV, SSD_CONV_DIM), f32) * SSD_CONV ** -0.5,
        "ssd_conv_b": 0.02 * nrm(ks[15], (N_C, SSD_CONV_DIM), f32),
        "ssd_dt_bias": dt + jnp.log(-jnp.expm1(-dt)),
        "ssd_a_log": jnp.log(jax.random.uniform(ks[16], (N_C, SSD_HEADS), f32, 1.0, 16.0)),
        "ssd_d": 1.0 + 0.02 * nrm(ks[17], (N_C, SSD_HEADS), f32),
        "ssd_norm_g": 1.0 + 0.02 * nrm(ks[18], (N_C, SSD_INNER), f32),
        "ssd_w_o": nrm(ks[19], (N_C, SSD_INNER, d), f32) * SSD_INNER ** -0.5,
        "mlp_w_in": nrm(ks[20], (DEPTH, d, MLP_HIDDEN), f32) * d ** -0.5,
        "mlp_w_out": nrm(ks[21], (DEPTH, MLP_HIDDEN, d), f32) * MLP_HIDDEN ** -0.5,
    }

def first_block(x, norm_mix_g, norm_mlp_g, sb_w_qkv, sb_q_norm_g, sb_k_norm_g, sb_w_o,
              gm_w_in, gm_v_norm_g, gm_w_s, gm_b_s, gm_w_o,
              ssd_w_in, ssd_conv_w, ssd_conv_b, ssd_dt_bias, ssd_a_log, ssd_d, ssd_norm_g, ssd_w_o,
              mlp_w_in, mlp_w_out):
    h = x
    for i in range(DEPTH):
        kind, j = i % N_MIXERS, i // N_MIXERS
        hn = rms_norm(h, norm_mix_g[i])
        if kind == 0:
            mix = stick_breaking_attention(hn, sb_w_qkv[j], sb_q_norm_g[j], sb_k_norm_g[j], sb_w_o[j])
        elif kind == 1:
            mix = chunked_spatial_gating(hn, gm_w_in[j], gm_v_norm_g[j], gm_w_s[j], gm_b_s[j], gm_w_o[j])
        else:
            mix = ssd_mixer(hn, ssd_w_in[j], ssd_conv_w[j], ssd_conv_b[j], ssd_dt_bias[j],
                            ssd_a_log[j], ssd_d[j], ssd_norm_g[j], ssd_w_o[j])
        h = h + mix
        h = h + squared_relu_mlp(rms_norm(h, norm_mlp_g[i]), mlp_w_in[i], mlp_w_out[i])
    return h


DEPTH_2 = 2

MIX = D_MODEL
D_MLA = MIX // 2
D_CONV = MIX - D_MLA
N_HEADS = 8
NOPE_DIM = 128
ROPE_DIM = 64
V_DIM = D_MLA // N_HEADS
QK_DIM = NOPE_DIM + ROPE_DIM
Q_LORA = 512
KV_LORA = 256
ROPE_THETA = 10000.0
CONV_K = 31
IN_COLS = Q_LORA + KV_LORA + ROPE_DIM + D_MLA + 2 * D_CONV + D_CONV


def rms_norm_2(x, g):
    xf = x.astype(jnp.float32)
    y = xf * lax.rsqrt(jnp.mean(xf * xf, axis=-1, keepdims=True) + EPS)
    return (y * g.astype(jnp.float32)).astype(x.dtype)

def layer_norm(x, g, b):
    xf = x.astype(jnp.float32)
    mu = jnp.mean(xf, axis=-1, keepdims=True)
    var = jnp.mean(jnp.square(xf - mu), axis=-1, keepdims=True)
    y = (xf - mu) * lax.rsqrt(var + EPS)
    return (y * g.astype(jnp.float32) + b.astype(jnp.float32)).astype(x.dtype)

def rope_tables(positions, dtype):
    inv_freq = 1.0 / (ROPE_THETA ** (jnp.arange(0, ROPE_DIM, 2, dtype=jnp.float32) / ROPE_DIM))
    ang = positions.astype(jnp.float32)[..., None] * inv_freq
    return jnp.cos(ang)[:, :, None, :].astype(dtype), jnp.sin(ang)[:, :, None, :].astype(dtype)

def apply_rope(x, cos, sin):
    x1, x2 = jnp.split(x, 2, axis=-1)
    return jnp.concatenate([x1 * cos - x2 * sin, x2 * cos + x1 * sin], axis=-1)

def causal_block_attention(q, k, v):
    b, s, h, dq = q.shape
    nb = s // Q_BLOCK
    scale = 1.0 / math.sqrt(dq)
    qb = q.reshape(b, nb, Q_BLOCK, h, dq).transpose(1, 0, 2, 3, 4)
    key_pos = jnp.arange(s)

    def one_block(args):
        q_i, blk = args
        scores = jnp.einsum('bqhd,bkhd->bhqk', q_i, k).astype(jnp.float32) * scale
        q_pos = blk * Q_BLOCK + jnp.arange(Q_BLOCK)
        mask = key_pos[None, :] <= q_pos[:, None]
        scores = jnp.where(mask[None, None], scores, -jnp.inf)
        p = jax.nn.softmax(scores, axis=-1).astype(v.dtype)
        return jnp.einsum('bhqk,bkhd->bqhd', p, v)

    out = lax.map(one_block, (qb, jnp.arange(nb)))
    return out.transpose(1, 0, 2, 3, 4).reshape(b, s, h, v.shape[-1])

def causal_depthwise_conv(u, w, bias):
    out = lax.conv_general_dilated(
        u, w[:, None, :].astype(u.dtype),
        window_strides=(1,), padding=((CONV_K - 1, 0),),
        dimension_numbers=('NWC', 'WIO', 'NWC'),
        feature_group_count=u.shape[-1])
    return out + bias

def second_inputs(seed: int = 0) -> dict:
    key = jax.random.key(seed)
    ks = jax.random.split(key, 24)
    f32 = jnp.float32

    def w(k, shape, fan_in):
        return jax.random.normal(k, shape, f32) * (fan_in ** -0.5)

    def gain(k, shape):
        return 1.0 + 0.05 * jax.random.normal(k, shape, f32)

    def small(k, shape):
        return 0.02 * jax.random.normal(k, shape, f32)

    x = jax.random.normal(ks[0], (BATCH, SEQ, D_MODEL), f32)
    c = jax.random.normal(ks[1], (BATCH, D_MODEL), f32)
    offsets = jax.random.randint(ks[2], (BATCH, 1), 0, 1024, dtype=jnp.int32)
    positions = offsets + jnp.arange(SEQ, dtype=jnp.int32)[None, :]
    return {
        'x': x,
        'c': c,
        'positions': positions,
        'ada_w': w(ks[3], (DEPTH_2, D_MODEL, 3 * D_MODEL), D_MODEL),
        'ada_b': small(ks[4], (DEPTH_2, 3 * D_MODEL)),
        'norm_g': gain(ks[5], (DEPTH_2, D_MODEL)),
        'w_in': w(ks[6], (DEPTH_2, D_MODEL, IN_COLS), D_MODEL),
        'q_lat_g': gain(ks[7], (DEPTH_2, Q_LORA)),
        'w_q_up': w(ks[8], (DEPTH_2, Q_LORA, N_HEADS * QK_DIM), Q_LORA),
        'kv_lat_g': gain(ks[9], (DEPTH_2, KV_LORA)),
        'w_kv_up': w(ks[10], (DEPTH_2, KV_LORA, N_HEADS * (NOPE_DIM + V_DIM)), KV_LORA),
        'q_norm_g': gain(ks[11], (DEPTH_2, QK_DIM)),
        'k_norm_g': gain(ks[12], (DEPTH_2, QK_DIM)),
        'glu_b': small(ks[13], (DEPTH_2, 2 * D_CONV)),
        'dw_w': w(ks[14], (DEPTH_2, CONV_K, D_CONV), CONV_K),
        'dw_b': small(ks[15], (DEPTH_2, D_CONV)),
        'conv_ln_g': gain(ks[16], (DEPTH_2, D_CONV)),
        'conv_ln_b': small(ks[17], (DEPTH_2, D_CONV)),
        'w_pw': w(ks[18], (DEPTH_2, D_CONV, D_CONV), D_CONV),
        'b_pw': small(ks[19], (DEPTH_2, D_CONV)),
        'w_out': w(ks[20], (DEPTH_2, MIX, D_MODEL), MIX),
    }

def second_block(x, c, positions, ada_w, ada_b, norm_g, w_in, q_lat_g, w_q_up, kv_lat_g,
              w_kv_up, q_norm_g, k_norm_g, glu_b, dw_w, dw_b, conv_ln_g, conv_ln_b,
              w_pw, b_pw, w_out):
    b, s, _ = x.shape
    cos, sin = rope_tables(positions, x.dtype)
    c_act = jax.nn.silu(c)
    splits = np.cumsum([Q_LORA, KV_LORA, ROPE_DIM, D_MLA, 2 * D_CONV]).tolist()

    for l in range(DEPTH_2):
        mod = c_act @ ada_w[l] + ada_b[l]
        shift, scale, gate = [m[:, None, :] for m in jnp.split(mod, 3, axis=-1)]
        h = rms_norm_2(x, norm_g[l]) * (1.0 + scale) + shift

        z = h @ w_in[l]
        q_lat, kv_lat, k_rope, mla_gate, conv_in, conv_gate = jnp.split(z, splits, axis=-1)

        q = (rms_norm_2(q_lat, q_lat_g[l]) @ w_q_up[l]).reshape(b, s, N_HEADS, QK_DIM)
        kv = (rms_norm_2(kv_lat, kv_lat_g[l]) @ w_kv_up[l]).reshape(b, s, N_HEADS, NOPE_DIM + V_DIM)
        k_nope, v = kv[..., :NOPE_DIM], kv[..., NOPE_DIM:]
        k_rope_h = jnp.broadcast_to(k_rope[:, :, None, :], (b, s, N_HEADS, ROPE_DIM))
        k = jnp.concatenate([k_nope, k_rope_h], axis=-1)
        q = rms_norm_2(q, q_norm_g[l])
        k = rms_norm_2(k, k_norm_g[l])
        q = jnp.concatenate([q[..., :NOPE_DIM], apply_rope(q[..., NOPE_DIM:], cos, sin)], axis=-1)
        k = jnp.concatenate([k[..., :NOPE_DIM], apply_rope(k[..., NOPE_DIM:], cos, sin)], axis=-1)
        attn = causal_block_attention(q, k, v).reshape(b, s, D_MLA)
        mla_out = attn * jax.nn.silu(mla_gate)

        u_val, u_gate = jnp.split(conv_in + glu_b[l], 2, axis=-1)
        u = u_val * jax.nn.sigmoid(u_gate)
        u = causal_depthwise_conv(u, dw_w[l], dw_b[l])
        u = jax.nn.silu(layer_norm(u, conv_ln_g[l], conv_ln_b[l]))
        u = u @ w_pw[l] + b_pw[l]
        conv_out = u * jax.nn.silu(conv_gate)

        y = jnp.concatenate([mla_out, conv_out], axis=-1) @ w_out[l]
        x = x + gate * y
    return x


def setup_inputs(seed=0):
    out = dict(first_inputs(seed))
    for name, value in second_inputs(seed + 1).items():
        if name != "x":
            out[name + "_2"] = value
    return out


def reference(
    x, norm_mix_g, norm_mlp_g, sb_w_qkv, sb_q_norm_g, sb_k_norm_g, sb_w_o, gm_w_in, gm_v_norm_g,
    gm_w_s, gm_b_s, gm_w_o, ssd_w_in, ssd_conv_w, ssd_conv_b, ssd_dt_bias, ssd_a_log, ssd_d,
    ssd_norm_g, ssd_w_o, mlp_w_in, mlp_w_out, c_2, positions_2, ada_w_2, ada_b_2, norm_g_2,
    w_in_2, q_lat_g_2, w_q_up_2, kv_lat_g_2, w_kv_up_2, q_norm_g_2, k_norm_g_2, glu_b_2, dw_w_2,
    dw_b_2, conv_ln_g_2, conv_ln_b_2, w_pw_2, b_pw_2, w_out_2,
):
    x = first_block(
        x, norm_mix_g, norm_mlp_g, sb_w_qkv, sb_q_norm_g, sb_k_norm_g, sb_w_o, gm_w_in,
        gm_v_norm_g, gm_w_s, gm_b_s, gm_w_o, ssd_w_in, ssd_conv_w, ssd_conv_b, ssd_dt_bias,
        ssd_a_log, ssd_d, ssd_norm_g, ssd_w_o, mlp_w_in, mlp_w_out,
    )
    return second_block(
        x, c_2, positions_2, ada_w_2, ada_b_2, norm_g_2, w_in_2, q_lat_g_2, w_q_up_2,
        kv_lat_g_2, w_kv_up_2, q_norm_g_2, k_norm_g_2, glu_b_2, dw_w_2, dw_b_2, conv_ln_g_2,
        conv_ln_b_2, w_pw_2, b_pw_2, w_out_2,
    )


_drawn_inputs = setup_inputs


def setup_inputs(seed=0):
    import zlib

    import numpy as np

    out = dict(_drawn_inputs(seed))
    spreads = {}
    factors = {'norm_mix_g': 3.837,
     'norm_mlp_g': 3.291,
     'sb_q_norm_g': 8.0,
     'sb_k_norm_g': 8.0,
     'ada_b_2': 4.893,
     'norm_g_2': 3.779,
     'q_lat_g_2': 8.0,
     'kv_lat_g_2': 8.0,
     'q_norm_g_2': 8.0,
     'k_norm_g_2': 8.0,
     'glu_b_2': 8.0,
     'dw_b_2': 8.0,
     'conv_ln_g_2': 5.456,
     'conv_ln_b_2': 8.0,
     'b_pw_2': 8.0}
    for name, (base, spread) in spreads.items():
        noise = np.random.default_rng([zlib.crc32(name.encode()), seed]).standard_normal(out[name].shape)
        drawn = base * np.exp(spread * noise) if base else spread * noise
        out[name] = __import__('jax').numpy.asarray(drawn.astype(out[name].dtype))
    for name, factor in factors.items():
        out[name] = (out[name] * factor).astype(out[name].dtype)
    return out
```

```python
import numpy as np
import concourse.bass as bass
from concourse import mybir
from contextlib import ExitStack

F32 = mybir.dt.float32
F32R = mybir.dt.float32r
I32 = mybir.dt.int32
ALU = mybir.AluOpType
ACT = mybir.ActivationFunctionType
AXX = mybir.AxisListType.X
K = 1024
EPS = 1e-6
D = 2048
CONVP = 0


class Engine:

    def __init__(self, sem):
        self.sem, self.n, self.seen, self.ops = sem, 0, {}, []

    def wait(self, *tokens):
        for t in tokens:
            if isinstance(t, list):
                self.wait(*t)
            elif t is not None and self.seen.get(t[0], 0) < t[1]:
                self.seen[t[0]] = t[1]
                self.ops.append(lambda e, s=t[0], v=t[1]: e.wait_ge(s, v))

    def do(self, fn, *after, inc=True):
        self.wait(*after)
        if inc:
            self.n += 1
            self.ops.append(lambda e: fn(e).then_inc(self.sem, 1))
            return (self.sem, self.n)
        self.ops.append(fn)
        return None

    def last(self):
        return (self.sem, self.n) if self.n else None


class Slots:

    def __init__(self, n):
        self.n, self.i, self.rel = n, 0, [[] for _ in range(n)]

    def take(self):
        s = self.i % self.n
        self.i += 1
        assert self.rel[s] is not None, "slot still held"
        w, self.rel[s] = self.rel[s], None
        return s, w

    def release(self, s, *tokens):
        self.rel[s] = list(tokens)


def build(nc, A, out):
    ctx = ExitStack()
    with ctx:
        sem = lambda n: ctx.enter_context(nc.semaphore(n))
        PE, SC, VE, PO, SP = (Engine(sem("s_" + n)) for n in ("pe", "act", "dve", "pool", "sp"))
        base = 16512
        at = [base]

        def put(name, shape, dt=F32, off=None):
            size = int(np.prod(shape[1:])) * 4
            if off is None:
                off = at[0]
                at[0] += (size + 31) // 32 * 32
            return nc.alloc_sbuf_tensor_at(name, shape, dt, offset=off)

        NR, NH, LA = 6, 4, 3
        RAW = put("RAW", [128, NR, 1024])
        WH = put("WH", [128, NH, 1024], F32R)
        WL = put("WL", [128, NH, 1024], F32R)
        X = put("X", [128, 2, D])
        oA = at[0]
        AH = put("AH", [128, 16, 256], F32R)
        AL = put("AL", [128, 16, 256], F32R)
        oBH = at[0]
        BH = put("BH", [128, 16, 256], F32R)
        oBL = at[0]
        BL = put("BL", [128, 16, 256], F32R)
        FB = put("FB", [128, 4, 512])
        CST = put("CST", [128, 6 * 128 + 32 + 1])
        VC = put("VC", [128, 3 * 128])
        DW = put("DW", [128, 2, 8, 31])
        MOD = put("MOD", [128, 2, 48])
        TRG = put("TRG", [128, 4, 64])
        CS = put("CS", [128, 2, 2, 32])
        TQ = put("TQ", [128, 4, 2, 32])
        TK = put("TK", [128, 4, 2, 32])
        CC = put("CC", [128, 16])
        ST = put("ST", [128, 64])
        SCL = put("SCL", [128, 16])
        GQ = put("GQ", [128, 4])
        oS = at[0]
        assert oS + 9152 + 44 * K <= 229344, (229344 - oS) / K

        IDN = CST[:, 0:128]
        MS = CST[:, 128:256]
        UN = CST[:, 256:384]
        NG = CST[:, 384:512]
        NM = CST[:, 512:640]
        ONE = CST[:, 640:768]
        INVF = CST[:, 768:800]
        MH = CST[:, 800:801]

        N = put("N", [128, 2, D], off=oS)
        QK = put("QK", [128, 2, 2, 512], off=oS)
        SQ = put("SQ", [128, 1024], off=oS + 8 * K)
        V1 = put("V1", [128, 2, 512], off=oS + 12 * K)
        QT1 = put("QT1", [128, 2, 4, 256], off=oS + 16 * K)
        TL = put("TL", [128, 4, 384], off=oS + 24 * K)
        TA = put("TA", [128, 4, 384], off=oS + 30 * K)
        TN = put("TN", [128, 4, 384], off=oS + 36 * K)
        ACC2 = put("ADA", [128, 2, 1024], off=oS + 44 * K)
        RN = put("RN", [128, 2, 2, 512], off=oS + 16 * K)
        VR = put("VR", [128, 3, 128], off=oS + 24 * K)
        DR = put("DR", [31, 2, 1024], off=oS + 26 * K)
        PI = put("PI", [128, 2], I32, off=oS + 34 * K)
        AG = put("AG", [128, 8, 64], off=oS + 35 * K)
        UT = put("UT", [128, 8, 286], off=oS)
        LNS = put("LNS", [128, 4, 256], off=oS)
        o2 = oS + 9152
        SMG = put("SMG", [128, 2, 1024], off=o2)
        SCG = put("SCG", [128, 2, 1024], off=o2 + 8 * K)
        KLH = put("KLH", [128, 2, 256], F32R, off=o2 + 16 * K)
        KLL = put("KLL", [128, 2, 256], F32R, off=o2 + 18 * K)
        KV = put("KV", [128, 2, 512], off=o2 + 20 * K)
        QN = put("QN", [128, 2, 384], off=o2 + 24 * K)
        QR = put("QR", [128, 4, 64], off=o2 + 27 * K)
        KR2 = put("KR2", [128, 4, 64], off=o2 + 28 * K)
        TT = put("TTr", [128, 4, 512], off=o2 + 29 * K)
        SCO = put("SCO", [128, 2, 384], off=o2 + 37 * K)
        PTB = put("PTB", [128, 2, 384], off=o2 + 40 * K)
        KR = put("KR", [128, 2, 64], off=o2 + 43 * K)
        RK = put("RK", [128, 2, 64], off=o2 + 43 * K + 512)
        ULH = put("ULH", [128, 8, 256], F32R, off=oA)
        ULL = put("ULL", [128, 8, 256], F32R, off=oA + 8 * K)
        G = put("G", [128, D], off=oA + 16 * K)
        MP = put("MP", [128, 2, 512], off=oA + 24 * K)
        BR = put("BR", [1, 1024], off=oA + 28 * K)
        UV = put("UV", [128, 2, 512], off=oBH)
        UG = put("UG", [128, 2, 512], off=oBH + 4 * K)
        CA = put("CA", [128, 8, 256], off=oBH + 8 * K)
        NQ = put("NQ", [128, 2, 512], off=oBL)
        NK = put("NK", [128, 2, 256], off=oBL + 4 * K)
        QLH = put("QLH", [128, 4, 256], F32R, off=oBL + 8 * K)
        QLL = put("QLL", [128, 4, 256], F32R, off=oBL + 12 * K)

        P = ctx.enter_context(nc.psum_tensor("P", [128, 8, 512], F32))

        f_slots = Slots(4)
        t_slots = Slots(4)
        pairs = Slots(2)

        def bank():
            s, w = t_slots.take()
            return s, P[:, 4 + s, :], w

        def fence():
            marks = [e.last() for e in (PE, SC, VE, PO)]
            for e in (PE, SC, VE, PO):
                e.wait(*marks)

        def copy_act(o, i, *w):
            return SC.do(lambda e: e.activation(o, i, ACT.Copy), *w)

        def copy_dve(o, i, *w):
            return VE.do(lambda e: e.tensor_copy(o, i), *w)

        def act(o, i, f, *w, **k):
            return SC.do(lambda e: e.activation(o, i, f, **k), *w)

        def tt(E, o, a, b, op, *w):
            return E.do(lambda e: e.tensor_tensor(o, a, b, op), *w)

        def ts(E, o, a, s1, s2, op0, op1, *w):
            if s2 is None:
                return E.do(lambda e: e.tensor_scalar(o, a, s1, None, op0), *w)
            return E.do(lambda e: e.tensor_scalar(o, a, s1, s2, op0, op1), *w)

        def stt(o, a, s, b, op0, op1, *w):
            return VE.do(lambda e: e.scalar_tensor_tensor(out=o, in0=a, scalar=s, in1=b, op0=op0, op1=op1), *w)

        def red(o, a, op, *w):
            return VE.do(lambda e: e.tensor_reduce(o, a, AXX, op), *w)

        def mm(o, l, r, st, sp, *w, inc=False, **k):
            return PE.do(lambda e: e.matmul(o, l, r, start=st, stop=sp, **k), *w, inc=inc)

        def tr(o, i, ident, *w, inc=False):
            return PE.do(lambda e: e.transpose(o, i, ident), *w, inc=inc)

        def power(o, ms, n, *w):
            return tt(PO, o, ms, MH.to_broadcast([128, n]), ALU.pow, *w)

        def split(f, fs, tok, H, L, *w):
            th = copy_act(H, f, tok, *w)
            tl = tt(VE, L, f, H.bitcast(F32), ALU.subtract, th, tok, *w)
            f_slots.release(fs, tl)
            return tl

        def flip(src, kts, wsrc, done, H, L, evac, *w):
            b, pb, wb = bank()
            for i, kt in enumerate(kts):
                for t in range(2):
                    last = tr(pb[:, (2 * i + t) * 128:(2 * i + t + 1) * 128], src(kt, t), IDN, wb, wsrc, c_tok,
                              inc=(i == 1 and t == 1))
            fs, wf = f_slots.take()
            f = FB[:, fs, :]
            te = evac(f, pb, kts, [last, wf])
            t_slots.release(b, te)
            tl = split(f, fs, te, H, L, *w)
            for kt in kts:
                done[kt] = tl
            return last, tl

        def affine(s, b):
            def go(f, pb, kts, w):
                for i, kt in enumerate(kts):
                    o, q = f[:, i * 256:(i + 1) * 256], pb[:, i * 256:(i + 1) * 256]
                    if b is None:
                        te = ts(VE, o, q, s[:, kt:kt + 1], None, ALU.mult, None, w)
                    else:
                        te = ts(VE, o, q, s[:, kt:kt + 1], b[:, kt:kt + 1], ALU.mult, ALU.add, w)
                return te
            return go

        def plain(f, pb, kts, w):
            return copy_act(f, pb, w)

        def squared(f, pb, kts, w):
            return act(f, pb, ACT.Square, w)

        s_c, s_x, s_v, s_br = sem("s_c"), sem("s_x"), sem("s_v"), sem("s_br")
        c_tok, x_tok = (s_c, 16), (s_x, 16)
        SP.ops.append(lambda e: e.dma_start(CST[:, :], A["consts"]).then_inc(s_c, 16))
        SP.ops.append(lambda e: e.dma_start(X[:, :, :], A["x"][0].rearrange("(t p) d -> p t d", p=128)).then_inc(s_x, 16))
        rows = [[("norm_mix_g", 16), ("norm_mlp_g", 16), ("norm_g_2", 32), ("q_lat_g_2", 8), ("kv_lat_g_2", 4),
                 ("conv_ln_g_2", 16), ("conv_ln_b_2", 16), ("sb_q_norm_g", 1), ("sb_k_norm_g", 1),
                 ("q_norm_g_2", 2), ("k_norm_g_2", 2)],
                [("dw_b_2", 16), ("glu_b_2", 32), ("c_2", 16)], [("ada_b_2", 96)]]
        col, nrow, nv = {}, [0, 0, 0], 0

        def vload(dst, src, **k):
            SC.ops.append(lambda e: e.dma_start(dst, src, **k).then_inc(s_v, 16))

        for g, names in enumerate(rows):
            for name, n in names:
                r = nrow[g]
                src = A[name][:, 0:128] if name in ("q_norm_g_2", "k_norm_g_2") else A[name].rearrange("a (r p) -> (a r) p", p=128)
                vload(VR[r:r + n, g, :], src)
                nv += 1
                col[name] = VC[:, g * 128 + r:g * 128 + r + n]
                nrow[g] = r + n
        vload(DR[:, :, :], A["dw_w_2"].rearrange("l k c -> k l c"))
        vload(PI[:, :], A["positions_2"].rearrange("a (t p) -> p (a t)", p=128), allow_slow_non_contiguous=True)
        for l in range(2):
            vload(TRG[:, 2 * l, :], A["q_norm_g_2"][l:l + 1, 128:192].to_broadcast([128, 64]))
            vload(TRG[:, 2 * l + 1, :], A["k_norm_g_2"][l:l + 1, 128:192].to_broadcast([128, 64]))
        nv += 6
        v_tok = (s_v, 16 * nv)

        b, pb, wb = bank()
        for g in range(3):
            n = nrow[g]
            last = tr(pb[:, g * 128:g * 128 + n], VR[0:n, g, :], CST[0:n, 0:n], v_tok, c_tok, inc=(g == 2))
        for g in range(3):
            vc_tok = copy_dve(VC[:, g * 128:g * 128 + nrow[g]], pb[:, g * 128:g * 128 + nrow[g]], last)
        t_slots.release(b, vc_tok)
        b, pb, wb = bank()
        for l in range(2):
            for c in range(8):
                o = (l * 8 + c) * 31
                last = tr(pb[:, o:o + 31], DR[0:31, l, c * 128:(c + 1) * 128], CST[0:31, 0:31], v_tok, inc=(l == 1 and c == 7))
        dw_tok = copy_dve(DW[:, :, :, :].rearrange("p a b c -> p (a b c)"), pb[:, 0:496], last)
        t_slots.release(b, dw_tok)
        gq_tok = ts(VE, GQ[:, 0:1], col["sb_q_norm_g"], 128.0 ** -0.5, None, ALU.mult, None, vc_tok)
        gq_tok = tt(VE, GQ[:, 1:3], col["q_norm_g_2"], col["k_norm_g_2"], ALU.mult, vc_tok)
        cc_tok = act(CC[:, :], col["c_2"], ACT.Silu, vc_tok)

        posf, ang, kk = AG[:, 0, 0:2], AG[:, 1, :], AG[:, 2, :]
        t0 = copy_dve(posf, PI[:, :], v_tok)
        for t in range(2):
            t1 = ts(VE, ang[:, 32 * t:32 * t + 32], INVF, posf[:, t:t + 1], None, ALU.mult, None, t0, c_tok)
        t1 = ts(VE, kk, ang, float(np.float32(1 / (2 * np.pi))), None, ALU.mult, None, t1)
        t1 = ts(VE, kk, kk, 12582912.0, None, ALU.add, None, t1)
        t1 = ts(VE, kk, kk, -12582912.0, None, ALU.add, None, t1)
        r1, cur = 2 * np.pi, ang
        for i in range(3):
            part = np.float32(r1)
            if i < 2:
                part = np.uint32(part.view(np.uint32) & np.uint32(0xFFFF8000)).view(np.float32)
            r1 -= float(part)
            t1 = stt(AG[:, 3 + i, :], kk, -float(part), cur, ALU.mult, ALU.add, t1)
            cur = AG[:, 3 + i, :]
        t1 = ts(VE, cur, cur, float(np.float32(3.1415925)), float(np.float32(-3.1415925)), ALU.min, ALU.max, t1)
        sv = CS[:, 1, :, :].rearrange("p t f -> p (t f)")
        cv = CS[:, 0, :, :].rearrange("p t f -> p (t f)")
        ta = act(sv, cur, ACT.Sin, t1)
        t2 = ts(VE, AG[:, 6, :], cur, -1.0, None, ALU.mult, None, t1)
        t2 = tt(VE, AG[:, 7, :], cur, AG[:, 6, :], ALU.max, t2)
        t2 = ts(VE, AG[:, 6, :], AG[:, 7, :], -1.0, float(np.float32(np.pi / 2)), ALU.mult, ALU.add, t2)
        cs_tok = act(cv, AG[:, 6, :], ACT.Sin, t2)

        class Gemm:
            def __init__(self, H, L, done):
                self.H, self.L, self.done, self.tok, self.bias, self.fence = H, L, done, {}, None, None
                self.end, self.last_unit, self.pair = None, None, {}

        plan = []

        def unit(g, c, src, r0, k0, nk, c0, w, st, sp):
            plan.append(dict(g=g, c=c, src=src, r0=r0, k0=k0, nk=nk, c0=c0, w=w, st=st, sp=sp))

        jobs = []

        def spawn(gen):
            jobs.append(gen)

        def pump():
            for j in list(jobs):
                try:
                    next(j)
                except StopIteration:
                    jobs.remove(j)

        raw_sem = [sem(f"s_raw{i}") for i in range(NR)]
        items, raw_free, state = [], {}, dict(dma=0, item=0)
        hl_slots = Slots(NH)
        wtok = {}

        def issue_dma():
            i = state["dma"]
            if i >= len(items):
                return
            state["dma"] += 1
            kind, u = items[i]
            s = i % NR
            SP.wait(raw_free.get(i - NR))
            if kind == "w":
                dst = RAW[:, s, 0:u["nk"] * u["w"]].rearrange("p (k n) -> p k n", k=u["nk"])
                src = u["src"][u["r0"]:u["r0"] + 128 * u["nk"], u["c0"]:u["c0"] + u["w"]].rearrange("(k p) n -> p k n", p=128)
            else:
                l, pc, kt = u
                dst = RAW[:, s, :]
                src = A["ada_w_2"][l, kt * 128:(kt + 1) * 128, pc * 1024:(pc + 1) * 1024]
            SP.ops.append(lambda e: e.dma_start(dst, src).then_inc(raw_sem[s], 16))

        ada_slots = Slots(2)
        ada = dict(tok=None, slot=0, w=None)
        mod_tok = {}

        def ada_reduce(l, pc, slot, tok):
            b, pb, wb = bank()
            for j in range(8):
                last = mm(pb[:, j:j + 1], ACC2[:, slot, j * 128:(j + 1) * 128], ONE[:, 0:1], True, True, wb, tok, c_tok, inc=(j == 7))
            ada_slots.release(slot, last)
            o = 8 * pc
            te = tt(VE, MOD[:, l, o:o + 8], pb[:, 0:8], col["ada_b_2"][:, 48 * l + o:48 * l + o + 8], ALU.add, last, vc_tok)
            t_slots.release(b, te)
            mod_tok[l] = te
            yield

        def take_item():
            i = state["item"]
            state["item"] += 1
            kind, u = items[i]
            s = i % NR
            there = (raw_sem[s], 16 * (i // NR + 1))
            if kind == "a":
                l, pc, kt = u
                if kt == 0:
                    ada["slot"], ada["w"] = ada_slots.take()
                acc = ACC2[:, ada["slot"], :]
                sc = CC[:, kt:kt + 1]
                if kt == 0:
                    t = ts(VE, acc, RAW[:, s, :], sc, None, ALU.mult, None, there, ada["w"], cc_tok)
                else:
                    t = stt(acc, RAW[:, s, :], sc, acc, ALU.mult, ALU.add, there, ada["tok"])
                ada["tok"] = t
                raw_free[i] = t
                if kt == 15:
                    spawn(ada_reduce(l, pc, ada["slot"], t))
            else:
                n = u["nk"] * u["w"]
                h, wh = hl_slots.take()
                r, H, L = RAW[:, s, 0:n], WH[:, h, 0:n], WL[:, h, 0:n]
                th = copy_act(H, r, there, wh)
                tl = tt(VE, L, r, H.bitcast(F32), ALU.subtract, there, th)
                raw_free[i] = tl
                wtok[id(u)] = (h, tl, th)
            issue_dma()
            return kind

        def run():
            w_at = [0]

            def prefetch(to):
                while w_at[0] < min(to, len(plan)):
                    if take_item() == "w":
                        w_at[0] += 1

            for i, u in enumerate(plan):
                prefetch(i + 1 + LA)
                g = u["g"]
                for k in range(u["nk"]):
                    while u["k0"] + k not in g.tok:
                        assert jobs
                        pump()
                if u["st"]:
                    while pairs.rel[pairs.i % 2] is None:
                        pump()
                    p, wp = pairs.take()
                    g.pair[u["c"]] = p
                    PE.wait(wp)
                p = g.pair[u["c"]]
                st = u["st"]
                if st and g.bias:
                    for t in range(2):
                        g.bias(P[:, 2 * p + t, 0:u["w"]], u["c"])
                    st = False
                h, tl, th = wtok[id(u)]
                W = u["w"]
                PE.wait(th, tl)
                for k in range(u["nk"]):
                    kt = u["k0"] + k
                    PE.wait(g.tok[kt])
                    wh, wl = WH[:, h, k * W:(k + 1) * W], WL[:, h, k * W:(k + 1) * W]
                    for t in range(2):
                        o = P[:, 2 * p + t, 0:W]
                        xh, xl = g.H[:, kt, t * 128:(t + 1) * 128], g.L[:, kt, t * 128:(t + 1) * 128]
                        end = k == u["nk"] - 1
                        mm(o, xh, wh, st and k == 0, False)
                        mm(o, xh, wl, False, False)
                        last = mm(o, xl, wh, False, u["sp"] and end, inc=(end and t == 1))
                hl_slots.release(h, last)
                g.end = last
                if u["sp"]:
                    spawn(g.done(u["c"], p, last))
                pump()
                if g.fence and i + 1 < len(plan) and u is g.last_unit:
                    g.fence()
            while jobs:
                pump()

        xs = {}

        def xw():
            return [x_tok] + list(xs.values())

        def xprep(dst, scale, bias, *w):
            fence()
            ta = act(N[:, 0, :], X[:, 0, :], ACT.Square, xw(), accum_out=ST[:, 0:1])
            tb = VE.do(lambda e: e.tensor_tensor_reduce(out=N[:, 1, :], in0=X[:, 1, :], in1=X[:, 1, :], scale=1.0, scalar=0.0,
                                                       op0=ALU.mult, op1=ALU.add, accum_out=ST[:, 1:2]), xw())
            t = ts(VE, ST[:, 2:4], ST[:, 0:2], 1.0 / D, EPS, ALU.mult, ALU.add, ta, tb)
            t = power(ST[:, 4:6], ST[:, 2:4], 2, t, c_tok)
            nt = {}
            for j in range(4):
                for tk in range(2):
                    nt[j] = ts(VE, N[:, tk, j * 512:(j + 1) * 512], X[:, tk, j * 512:(j + 1) * 512], ST[:, 4 + tk:5 + tk], None,
                               ALU.mult, None, t)
                for k in (4 * j, 4 * j + 2):
                    last, tl = flip(lambda kt, tk: N[:, tk, kt * 128:(kt + 1) * 128], (k, k + 1), nt[j], dst.tok,
                                    dst.H[:, k:k + 2, :].rearrange("p a b -> p (a b)"), dst.L[:, k:k + 2, :].rearrange("p a b -> p (a b)"),
                                    affine(scale, bias), *w)
            fence()
            yield

        qkt = dict(nat=[None, None], T=[None, None], rT=[None, None], V=None, rV=None)
        wo_tok = {}

        def qkv_done(c, p, tok):
            j, kind = c // 3, c % 3
            if kind == 2:
                for t in range(2):
                    te = copy_act(V1[:, t, :], P[:, 2 * p + t, :], tok, qkt["rV"])
                pairs.release(p, te)
                qkt["V"] = te
                spawn(sb_heads(j, 0))
                spawn(sb_heads(j, 1))
                return
            nat = QK[:, kind, :, :].rearrange("p t n -> p (t n)")
            for t in range(2):
                te = copy_act(QK[:, kind, t, :], P[:, 2 * p + t, :], tok, qkt["nat"][kind])
            pairs.release(p, te)
            n8 = nat.rearrange("p (a d) -> p a d", d=128)
            q = tt(PO, SQ[:, :], nat, nat, ALU.mult, te)
            o = 8 + 24 * kind
            q = red(ST[:, o:o + 8], SQ[:, :].rearrange("p (a d) -> p a d", d=128), ALU.add, q)
            q = ts(VE, ST[:, o + 8:o + 16], ST[:, o:o + 8], 1.0 / 128, EPS, ALU.mult, ALU.add, q)
            yield
            q = power(ST[:, o + 16:o + 24], ST[:, o + 8:o + 16], 8, q)
            q = tt(PO, n8, n8, ST[:, o + 16:o + 24].rearrange("p (a b) -> p a b", b=1).to_broadcast([128, 8, 128]), ALU.mult, q)
            yield
            sc = GQ[:, 0:1] if kind == 0 else col["sb_k_norm_g"]
            for hp in range(2):
                b, pb, wb = bank()
                for h in range(2):
                    for t in range(2):
                        last = tr(pb[:, (2 * h + t) * 128:(2 * h + t + 1) * 128], QK[:, kind, t, (2 * hp + h) * 128:(2 * hp + h + 1) * 128],
                                  IDN, wb, q, inc=(h == 1 and t == 1))
                te = act(QT1[:, kind, 2 * hp:2 * hp + 2, :].rearrange("p a b -> p (a b)"), pb, ACT.Copy, last, gq_tok, vc_tok,
                         qkt["rT"][kind], scale=sc)
                t_slots.release(b, te)
            qkt["nat"][kind] = last
            qkt["T"][kind] = te

        tl_rel = [None, None]

        def sb_heads(j, hp):
            while None in qkt["T"]:
                yield
            sl, t1s, nls = [], [], []
            for i in range(2):
                h, s = 2 * hp + i, 2 * hp + i
                b, pb, wb = bank()
                mm(pb[:, 0:256], QT1[:, 1, h, 0:128], QT1[:, 0, h, :], True, True, wb, qkt["T"])
                last = mm(pb[:, 256:384], QT1[:, 1, h, 128:256], QT1[:, 0, h, 128:256], True, True, inc=True)
                z = pb[:, 0:384]
                t = act(TL[:, s, :], z, ACT.Abs, last, tl_rel[hp])
                t = act(TL[:, s, :], TL[:, s, :], ACT.Exp, t, scale=-1.0)
                t = act(TL[:, s, :], TL[:, s, :], ACT.Ln, t, bias=1.0)
                t1 = stt(TA[:, s, :], z, 0.0, TL[:, s, :], ALU.min, ALU.subtract, t, tl_rel[hp])
                t2 = stt(TN[:, s, :], z, 0.0, TL[:, s, :], ALU.max, ALU.add, t, tl_rel[hp])
                t_slots.release(b, t2)
                nd = TN[:, s, :].rearrange("p (a b) -> p a b", b=128)[:, 0:3:2, :]
                t3 = tt(PO, nd, nd, MS.rearrange("p (a b) -> p a b", a=1).to_broadcast([128, 2, 128]), ALU.mult, t2)
                t1s.append(t1)
                nls.append(t3)
            qkt["rT"] = [last, last]
            yield
            as_ = []
            for i in range(2):
                s = 2 * hp + i
                b, pb, wb = bank()
                mm(pb[:, 0:128], UN, TN[:, s, 0:128], True, True, wb, nls[i])
                mm(pb[:, 128:256], UN, TN[:, s, 128:256], True, False)
                mm(pb[:, 128:256], NG, TN[:, s, 256:384], False, True)
                last = mm(pb[:, 256:384], UN, TN[:, s, 256:384], True, True, inc=True)
                t = tt(VE, TA[:, s, :], pb[:, 0:384], TA[:, s, :], ALU.add, last, t1s[i])
                t_slots.release(b, t)
                t = act(TA[:, s, :], TA[:, s, :], ACT.Exp, t)
                ad = TA[:, s, :].rearrange("p (a b) -> p a b", b=128)[:, 0:3:2, :]
                as_.append(tt(PO, ad, ad, MS.rearrange("p (a b) -> p a b", a=1).to_broadcast([128, 2, 128]), ALU.mult, t))
            yield
            b, pb, wb = bank()
            for i in range(2):
                h, s = 2 * hp + i, 2 * hp + i
                o = pb[:, i * 256:(i + 1) * 256]
                v0, v1 = V1[:, 0, h * 128:(h + 1) * 128], V1[:, 1, h * 128:(h + 1) * 128]
                mm(o[:, 0:128], v0, TA[:, s, 0:128], True, True, wb, as_[i], qkt["V"])
                mm(o[:, 128:256], v0, TA[:, s, 128:256], True, False)
                last = mm(o[:, 128:256], v1, TA[:, s, 256:384], False, True, inc=(i == 1))
            tl_rel[hp] = last
            qkt["rV"] = last
            fs, wf = f_slots.take()
            te = copy_act(FB[:, fs, :], pb, last, wf)
            t_slots.release(b, te)
            kt = 4 * j + 2 * hp
            tl = split(FB[:, fs, :], fs, te, BH[:, kt:kt + 2, :].rearrange("p a b -> p (a b)"), BL[:, kt:kt + 2, :].rearrange("p a b -> p (a b)"))
            g_wo.tok[kt] = g_wo.tok[kt + 1] = tl

        def add_x(c, p, tok):
            for t in range(2):
                o = X[:, t, c * 512:(c + 1) * 512]
                te = tt(VE, o, o, P[:, 2 * p + t, :], ALU.add, tok, xs.get((c, t)), x_tok)
                xs[(c, t)] = te
            pairs.release(p, te)
            return
            yield

        g_qkv = Gemm(AH, AL, qkv_done)
        g_wo = Gemm(BH, BL, add_x)

        g_m1 = Gemm(AH, AL, None)
        rn_slots = Slots(2)
        m2 = [Gemm(BH[:, 8 * (e % 2):8 * (e % 2) + 8, :], BL[:, 8 * (e % 2):8 * (e % 2) + 8, :], add_x) for e in range(8)]

        def m1_done(c, p, tok):
            e, cc = c // 2, c % 2
            s, ws = rn_slots.take()
            for t in range(2):
                te = act(RN[:, s, t, :], P[:, 2 * p + t, :], ACT.Relu, tok, ws)
            pairs.release(p, te)
            free = m2[e - 2].end if e >= 2 else g_wo.end
            yield
            for i in (0, 2):
                k = 4 * cc + i
                last, tl = flip(lambda kt, t: RN[:, s, t, (kt - 4 * cc) * 128:(kt - 4 * cc + 1) * 128], (k, k + 1), te, m2[e].tok,
                                m2[e].H[:, k:k + 2, :].rearrange("p a b -> p (a b)"), m2[e].L[:, k:k + 2, :].rearrange("p a b -> p (a b)"),
                                squared, free)
                if i == 2:
                    rn_slots.release(s, last)
                yield

        g_m1.done = m1_done

        def layer(l):
            gz = Gemm(AH, AL, None)
            gq = Gemm(QLH, QLL, None)
            gk = Gemm(KLH, KLL, None)
            gp = Gemm(ULH, ULL, None)
            go = Gemm(BH, BL, None)
            T = {}
            cgl = lambda name, n: col[name][:, n * l:n * l + n]

            def start():
                t = stt(SCL[:, :], MOD[:, l, 16:32], 1.0, cgl("norm_g_2", 16), ALU.add, ALU.mult, mod_tok[l], vc_tok, PE.last())
                yield from xprep(gz, SCL, MOD[:, l, 0:16])
                T["pad"] = VE.do(lambda e: e.memset(UT[:, :, 0:30], 0.0))
                for tab, gi in ((TQ, 2 * l), (TK, 2 * l + 1)):
                    for i, (gs, f) in enumerate(((0, 0), (32, 1), (32, 0), (0, 1))):
                        T["tab"] = tt(PO, tab[:, i, :, :], CS[:, f, :, :],
                                      TRG[:, gi:gi + 1, gs:gs + 32].to_broadcast([128, 2, 32]), ALU.mult, cs_tok, v_tok)

            uv = {}
            conv = {}

            def z_done(c, p, tok):
                pp = [P[:, 2 * p, :], P[:, 2 * p + 1, :]]
                if c in (0, 2):
                    for t in range(2):
                        te = copy_act(UV[:, t, :], pp[t], tok, T.get("uvr"))
                    pairs.release(p, te)
                    T["uv"] = te
                    return
                if c in (1, 3):
                    j = c // 2
                    for t in range(2):
                        te = copy_act(UG[:, t, :], pp[t], tok, T.get("uvr"))
                    pairs.release(p, te)
                    bg = cgl("glu_b_2", 16)
                    yield
                    for i in range(4):
                        ct = 4 * j + i
                        b, pb, wb = bank()
                        for t in range(2):
                            tr(pb[:, t * 128:(t + 1) * 128], UV[:, t, i * 128:(i + 1) * 128], IDN, wb, te, T["uv"])
                            last = tr(pb[:, 256 + t * 128:256 + (t + 1) * 128], UG[:, t, i * 128:(i + 1) * 128], IDN, inc=(t == 1))
                        fs, wf = f_slots.take()
                        ta = act(FB[:, fs, 0:256], pb[:, 256:512], ACT.Sigmoid, last, wf, bias=bg[:, 8 + ct:9 + ct])
                        tb = stt(UT[:, ct, 30:286], pb[:, 0:256], bg[:, ct:ct + 1], FB[:, fs, 0:256], ALU.add, ALU.mult, ta, T["pad"])
                        f_slots.release(fs, tb)
                        t_slots.release(b, tb)
                        conv[ct] = tb
                        if i % 2:
                            yield
                    T["uvr"] = last
                    spawn(convolve(range(4 * j, 4 * j + 4)))
                    return
                if c == 4:
                    for t in range(2):
                        te = copy_act(NQ[:, t, :], pp[t], tok)
                    pairs.release(p, te)
                    yield from latent(NQ, 512, te, 6, gq, QLH, QLL, cgl("q_lat_g_2", 4))
                    return
                if c == 5:
                    for t in range(2):
                        te = copy_act(NK[:, t, :], pp[t][:, 0:256], tok)
                        te = copy_act(KR[:, t, :], pp[t][:, 256:320], tok)
                    pairs.release(p, te)
                    q = tt(PO, FBk, KR[:, :, :], KR[:, :, :], ALU.mult, te)
                    T["ssr"] = red(ST[:, 56:58], FBk, ALU.add, q)
                    q = te
                    for t in range(2):
                        q = rope(RK[:, t:t + 1, :], KR[:, t:t + 1, :], TK, t, [1], q)
                    T["rk"] = q
                    yield from latent(NK, 256, te, 14, gk, KLH, KLL, cgl("kv_lat_g_2", 2))
                    return
                dst = SMG if c < 8 else SCG
                o = (c % 2) * 512
                for t in range(2):
                    te = act(dst[:, t, o:o + 512], pp[t], ACT.Silu, tok)
                pairs.release(p, te)
                T["g", c] = te

            FBk = UTk[:, :].rearrange("p (a b) -> p a b", a=2)

            def rope(o, x, tab, t, shape, *w):
                n = shape[0]
                tb = [tab[:, i, t:t + 1, :].to_broadcast([128, n, 32]) for i in range(4)]
                tm = RT[:, 0:4 * n * 32].rearrange("p (i a b) -> p i a b", i=4, a=n)
                x1, x2 = x[:, :, 0:32], x[:, :, 32:64]
                q0 = tt(PO, tm[:, 0, :, :], x1, tb[0], ALU.mult, T["tab"], *w)
                q1 = tt(PO, tm[:, 1, :, :], x2, tb[1], ALU.mult)
                q2 = tt(PO, tm[:, 2, :, :], x2, tb[2], ALU.mult)
                q3 = tt(PO, tm[:, 3, :, :], x1, tb[3], ALU.mult)
                q = tt(PO, o[:, :, 0:32], tm[:, 0, :, :], tm[:, 1, :, :], ALU.subtract, q1)
                return tt(PO, o[:, :, 32:64], tm[:, 2, :, :], tm[:, 3, :, :], ALU.add, q3)

            def latent(NAT, n, te, o, g, H, L, gain):
                for t in range(2):
                    fs, wf = f_slots.take()
                    q = act(FB[:, fs, 0:n], NAT[:, t, :], ACT.Square, te, wf, accum_out=ST[:, o + t:o + t + 1])
                    f_slots.release(fs, q)
                q = ts(VE, ST[:, o + 2:o + 4], ST[:, o:o + 2], 1.0 / n, EPS, ALU.mult, ALU.add, q)
                q = power(ST[:, o + 4:o + 6], ST[:, o + 2:o + 4], 2, q)
                yield
                for t in range(2):
                    q2 = ts(VE, NAT[:, t, :], NAT[:, t, :], ST[:, o + 4 + t:o + 5 + t], None, ALU.mult, None, q)
                yield
                for k in range(0, n // 128, 2):
                    flip(lambda kt, t: NAT[:, t, kt * 128:(kt + 1) * 128], (k, k + 1), q2, g.tok,
                         H[:, k:k + 2, :].rearrange("p a b -> p (a b)"), L[:, k:k + 2, :].rearrange("p a b -> p (a b)"), affine(gain, None))
                    yield

            def convolve(cts):
                per = 2
                ctok = {}
                for k in range(31):
                    for ct in cts:
                        x, w = UT[:, ct, k:k + 256], DW[:, l, ct, k:k + 1]
                        if k == 0:
                            ctok[ct] = ts(VE, CA[:, ct, :], x, w, cgl("dw_b_2", 8)[:, ct:ct + 1], ALU.mult, ALU.add, conv[ct], dw_tok)
                        else:
                            ctok[ct] = stt(CA[:, ct, :], x, w, CA[:, ct, :], ALU.mult, ALU.add, ctok[ct])
                    yield
                for ct in cts:
                    conv["d", ct] = ctok[ct]
                if all(("d", ct) in conv for ct in range(8)):
                    T["conv"] = [conv["d", ct] for ct in range(8)]

            def layernorm():
                b, pb, wb = bank()
                for ct in range(8):
                    last = mm(pb[:, 0:256], ONE, CA[:, ct, :], ct == 0, ct == 7, wb, T["conv"], inc=(ct == 7))
                mu = LNS[:, 0, :]
                t = ts(VE, mu, pb[:, 0:256], 1.0 / 1024, None, ALU.mult, None, last)
                t_slots.release(b, t)
                t = tt(VE, CA[:, :, :], CA[:, :, :], LNS[:, 0:1, :].to_broadcast([128, 8, 256]), ALU.subtract, t)
                yield
                b, pb, wb = bank()
                for cp in range(4):
                    fs, wf = f_slots.take()
                    q = act(FB[:, fs, :], CA[:, 2 * cp:2 * cp + 2, :].rearrange("p a b -> p (a b)"), ACT.Square, t, wf)
                    for i in range(2):
                        last = mm(pb[:, 0:256], ONE, FB[:, fs, i * 256:(i + 1) * 256], cp == 0 and i == 0, cp == 3 and i == 1, wb, q, inc=(i == 1))
                    f_slots.release(fs, last)
                q = ts(VE, LNS[:, 1, :], pb[:, 0:256], 1.0 / 1024, EPS, ALU.mult, ALU.add, last)
                t_slots.release(b, q)
                q = power(LNS[:, 2, :], LNS[:, 1, :], 256, q)
                yield
                q = tt(VE, CA[:, :, :], CA[:, :, :], LNS[:, 2:3, :].to_broadcast([128, 8, 256]), ALU.mult, q)
                lg, lb = cgl("conv_ln_g_2", 8), cgl("conv_ln_b_2", 8)
                for cp in range(4):
                    fs, wf = f_slots.take()
                    for i in range(2):
                        ct = 2 * cp + i
                        te = act(FB[:, fs, i * 256:(i + 1) * 256], CA[:, ct, :], ACT.Silu, q, wf, scale=lg[:, ct:ct + 1], bias=lb[:, ct:ct + 1])
                    tl = split(FB[:, fs, :], fs, te, ULH[:, 2 * cp:2 * cp + 2, :].rearrange("p a b -> p (a b)"),
                               ULL[:, 2 * cp:2 * cp + 2, :].rearrange("p a b -> p (a b)"))
                    gp.tok[2 * cp] = gp.tok[2 * cp + 1] = tl
                    yield

            att = dict(q=[], k=[], free_nat=None, freeT=None, freeKV=None)

            def q_done(g, p, tok):
                while att.get("busyq"):
                    yield
                att["busyq"] = True
                for t in range(2):
                    te = copy_act(QN[:, t, :], P[:, 2 * p + t, 0:384], tok, att.get("rq"))
                pairs.release(p, te)
                for t in range(2):
                    fs, wf = f_slots.take()
                    q = tt(PO, FB[:, fs, 0:384], QN[:, t, :], QN[:, t, :], ALU.mult, te, wf)
                    q = red(ST[:, 20 + 2 * t:22 + 2 * t], FB[:, fs, 0:384].rearrange("p (a d) -> p a d", a=2), ALU.add, q)
                    f_slots.release(fs, q)
                q = ts(VE, ST[:, 24:28], ST[:, 20:24], 1.0 / 192, EPS, ALU.mult, ALU.add, q)
                yield
                q = power(ST[:, 28:32], ST[:, 24:28], 4, q)
                x = QN[:, :, :].rearrange("p t (h d) -> p (t h) d", h=2)
                q = tt(PO, x, x, ST[:, 28:32].rearrange("p (a b) -> p a b", b=1).to_broadcast([128, 4, 192]), ALU.mult, q)
                for t in range(2):
                    q = rope(QR[:, 2 * t:2 * t + 2, :], x[:, 2 * t:2 * t + 2, 128:192], TQ, t, [2], q, att.get("rq"))
                yield
                att["qn"] = q

            def kv_done(g, p, tok):
                while att.get("busyk"):
                    yield
                att["busyk"] = True
                for t in range(2):
                    te = copy_act(KV[:, t, :], P[:, 2 * p + t, :], tok, att.get("rkv"))
                pairs.release(p, te)
                kv = KV[:, :, :].rearrange("p t (h d) -> p (t h) d", h=2)
                kn = kv[:, :, 0:128]
                fs, wf = f_slots.take()
                f4 = FB[:, fs, :].rearrange("p (a d) -> p a d", a=4)
                q = tt(PO, f4, kn, kn, ALU.mult, te, wf)
                q = red(ST[:, 32:36], f4, ALU.add, q)
                f_slots.release(fs, q)
                for t in range(2):
                    q2 = ts(VE, ST[:, 36 + 2 * t:38 + 2 * t], ST[:, 32 + 2 * t:34 + 2 * t], ST[:, 56 + t:57 + t], 1.0 / 192, ALU.add, ALU.mult, q, T["ssr"])
                q = ts(VE, ST[:, 36:40], ST[:, 36:40], EPS, None, ALU.add, None, q2)
                yield
                q = power(ST[:, 40:44], ST[:, 36:40], 4, q)
                q1 = tt(PO, kn, kn, ST[:, 40:44].rearrange("p (a b) -> p a b", b=1).to_broadcast([128, 4, 128]), ALU.mult, q)
                for t in range(2):
                    q1 = tt(PO, KR2[:, 2 * t:2 * t + 2, :], RK[:, t:t + 1, :].to_broadcast([128, 2, 64]),
                            ST[:, 40 + 2 * t:42 + 2 * t].rearrange("p (a b) -> p a b", b=1).to_broadcast([128, 2, 64]), ALU.mult, q, T["rk"],
                            att.get("rkr"))
                yield
                while "qn" not in att:
                    yield
                qn = att.pop("qn")
                tt_tok = []
                for which in range(4):
                    b, pb, wb = bank()
                    rows = 128 if which < 2 else 64
                    for h in range(2):
                        for t in range(2):
                            o = pb[0:rows, (2 * h + t) * 128:(2 * h + t + 1) * 128]
                            src = (QN[:, t, h * 192:h * 192 + 128], KV[:, t, h * 256:h * 256 + 128], QR[:, 2 * t + h, :], KR2[:, 2 * t + h, :])[which]
                            last = tr(o, src, IDN, wb, qn, q1, inc=(h == 1 and t == 1))
                    if which == 0:
                        te = ts(VE, TT[0:rows, which, :], pb[0:rows, :], GQ[:, 1 + l:2 + l], None, ALU.mult, None, last, att.get("rT"))
                    else:
                        te = copy_act(TT[0:rows, which, :], pb[0:rows, :], last, att.get("rT"))
                    tt_tok.append(te)
                    t_slots.release(b, te)
                att["rq"] = att["rkr"] = last
                att["busyq"] = False
                yield
                isc = 192.0 ** -0.5
                ex = []
                for h in range(2):
                    b, pb, wb = bank()
                    for t, (o, n) in enumerate(((0, 128), (128, 256))):
                        qs, ks = slice(h * 256 + t * 128, h * 256 + t * 128 + 128), slice(h * 256, h * 256 + n)
                        mm(pb[:, o:o + n], TT[:, 0, qs], TT[:, 1, ks], True, False, wb, tt_tok)
                        last = mm(pb[:, o:o + n], TT[0:64, 2, qs], TT[0:64, 3, ks], False, True, inc=(t == 1))
                    dg = SCO[:, h, :].rearrange("p (a b) -> p a b", b=128)[:, 0:3:2, :]
                    pd = pb[:, 0:384].rearrange("p (a b) -> p a b", b=128)[:, 0:3:2, :]
                    ta = tt(VE, dg, pd, NM.rearrange("p (a b) -> p a b", a=1).to_broadcast([128, 2, 128]), ALU.add, last, att.get("rS"))
                    tb = copy_dve(SCO[:, h, 128:256], pb[:, 128:256], last, att.get("rS"))
                    t_slots.release(b, tb)
                    m = ST[:, 44 + 2 * h:46 + 2 * h]
                    red(m[:, 0:1], SCO[:, h, 0:128], ALU.max, ta, tb)
                    tm = red(m[:, 1:2], SCO[:, h, 128:384], ALU.max, ta, tb)
                    tm = ts(VE, m, m, -isc, None, ALU.mult, None, tm)
                    act(SCO[:, h, 0:128], SCO[:, h, 0:128], ACT.Exp, tm, scale=isc, bias=m[:, 0:1], accum_out=ST[:, 48 + 2 * h:49 + 2 * h])
                    te = act(SCO[:, h, 128:384], SCO[:, h, 128:384], ACT.Exp, scale=isc, bias=m[:, 1:2], accum_out=ST[:, 49 + 2 * h:50 + 2 * h])
                    ex.append(te)
                ri = VE.do(lambda e: e.reciprocal(ST[:, 52:56], ST[:, 48:52]), ex)
                att["rT"] = last
                yield
                pt = []
                for h in range(2):
                    b, pb, wb = bank()
                    for i in range(3):
                        last = tr(pb[:, i * 128:(i + 1) * 128], SCO[:, h, i * 128:(i + 1) * 128], IDN, wb, ex[h], inc=(i == 2))
                    te = copy_act(PTB[:, h, :], pb[:, 0:384], last, att.get("rP"))
                    t_slots.release(b, te)
                    pt.append(te)
                att["rS"] = last
                yield
                while ("g", 6 + g // 2) not in T:
                    yield
                b, pb, wb = bank()
                for h in range(2):
                    v0, v1 = (KV[:, t, h * 256 + 128:h * 256 + 256] for t in range(2))
                    o0, o1 = (pb[:, (2 * t + h) * 128:(2 * t + h + 1) * 128] for t in range(2))
                    mm(o0, PTB[:, h, 0:128], v0, True, True, wb, pt)
                    mm(o1, PTB[:, h, 128:256], v0, True, False)
                    last = mm(o1, PTB[:, h, 256:384], v1, False, True, inc=(h == 1))
                att["rkv"] = att["rP"] = last
                fs, wf = f_slots.take()
                f = FB[:, fs, :]
                for t in range(2):
                    for h in range(2):
                        s = slice((2 * t + h) * 128, (2 * t + h + 1) * 128)
                        te = stt(f[:, s], pb[:, s], ST[:, 52 + 2 * h + t:53 + 2 * h + t], SMG[:, t, (2 * g + h) * 128:(2 * g + h + 1) * 128],
                                 ALU.mult, ALU.mult, last, wf, ri, T["g", 6 + g // 2])
                t_slots.release(b, te)
                yield
                flast, tl = flip(lambda kt, t: f[:, (2 * t + kt - 2 * g) * 128:(2 * t + kt - 2 * g + 1) * 128], (2 * g, 2 * g + 1), te, go.tok,
                                 BH[:, 2 * g:2 * g + 2, :].rearrange("p a b -> p (a b)"), BL[:, 2 * g:2 * g + 2, :].rearrange("p a b -> p (a b)"),
                                 plain)
                f_slots.release(fs, flast)
                att["busyk"] = False

            def after_z():
                fence()
                SC.ops.append(lambda e: e.dma_start(BR[0:1, :], A["b_pw_2"][l:l + 1, :]).then_inc(s_br, 16))
                while "conv" not in T:
                    yield
                yield from layernorm()
                for j in range(4):
                    b, pb, wb = bank()
                    for i in range(4):
                        gc = MOD[:, l, 32 + 4 * j + i:33 + 4 * j + i].to_broadcast([128, 128])
                        last = mm(pb[:, i * 128:(i + 1) * 128], gc, IDN, True, True, wb, inc=(i == 3))
                    T["G", j] = copy_act(G[:, j * 512:(j + 1) * 512], pb, last)
                    t_slots.release(b, T["G", j])
                    yield

            def p_done(c, p, tok):
                for t in range(2):
                    te = tt(VE, MP[:, t, :], P[:, 2 * p + t, :], SCG[:, t, c * 512:(c + 1) * 512], ALU.mult, tok, T["g", 8 + c], T.get("mp"))
                pairs.release(p, te)
                yield
                for i in (0, 2):
                    k = 8 + 4 * c + i
                    T["mp"], _ = flip(lambda kt, t: MP[:, t, (kt - 8 - 4 * c) * 128:(kt - 7 - 4 * c) * 128], (k, k + 1), te, go.tok,
                                      BH[:, k:k + 2, :].rearrange("p a b -> p (a b)"), BL[:, k:k + 2, :].rearrange("p a b -> p (a b)"), plain)
                    if i == 0:
                        yield

            def o_done(c, p, tok):
                for t in range(2):
                    fs, wf = f_slots.take()
                    te = tt(VE, FB[:, fs, :], P[:, 2 * p + t, :], G[:, c * 512:(c + 1) * 512], ALU.mult, tok, T["G", c], wf)
                    o = X[:, t, c * 512:(c + 1) * 512]
                    xs[(c, t)] = tx = tt(PO, o, o, FB[:, fs, :], ALU.add, te, xs[(c, t)])
                    f_slots.release(fs, tx)
                pairs.release(p, te)
                if l == 1:
                    for t in range(2):
                        SP.wait(xs[(c, t)])
                    SP.ops.append(lambda e: e.dma_start(out[0].rearrange("(t p) d -> p t d", p=128)[:, :, c * 512:(c + 1) * 512],
                                                        X[:, :, c * 512:(c + 1) * 512]).then_inc(s_out, 16))
                return
                yield

            def bias(o, c):
                mm(o, ONE[0:1, :], BR[0:1, c * 512:(c + 1) * 512], True, False, (s_br, 16 * (l + 1)))

            gz.done, gq.done, gk.done, gp.done, go.done = z_done, q_done, kv_done, p_done, o_done
            gp.bias = bias
            w_in, w_o = A["w_in_2"][l], A["w_out_2"][l]
            zc = [(1856, 512), (2880, 512), (2368, 512), (3392, 512), (0, 512), (512, 320), (832, 512), (1344, 512), (3904, 512), (4416, 512)]

            def z_units(c):
                c0, w = zc[c]
                for k in range(0, 16, 2):
                    unit(gz, c, w_in, k * 128, k, 2, c0, w, k == 0, k == 14)

            def up_units(g):
                for k in (0, 2):
                    unit(gq, g, A["w_q_up_2"][l], k * 128, k, 2, 384 * g, 384, k == 0, k == 2)
                unit(gk, g, A["w_kv_up_2"][l], 0, 0, 2, 512 * g, 512, True, True)

            for c in range(7):
                z_units(c)
            up_units(0)
            z_units(7)
            up_units(1)
            z_units(8)
            up_units(2)
            z_units(9)
            gz.last_unit = plan[-1]
            gz.fence = lambda: spawn(after_z())
            up_units(3)
            for c in range(2):
                for k in range(0, 8, 2):
                    unit(gp, c, A["w_pw_2"][l], k * 128, k, 2, 512 * c, 512, k == 0, k == 6)

            def o_units(c, ks):
                for k in ks:
                    unit(go, c, w_o, k * 128, k, 2, 512 * c, 512, k == 8, k == 6)

            o_units(0, (8, 10, 12, 14))
            o_units(1, (8, 10, 12, 14))
            o_units(0, (0, 2, 4, 6))
            o_units(1, (0, 2, 4, 6))
            for c in (2, 3):
                o_units(c, (8, 10, 12, 14, 0, 2, 4, 6))
            go.last_unit = plan[-1]
            return start, go

        s_out = sem("s_out")
        UTk = put("UTk", [128, 128], off=oBL + 6 * K)
        RT = put("RT", [128, 256], off=oBL + 6 * K + 512)

        wq, wo = A["sb_w_qkv"][0], A["sb_w_o"][0]
        for j in range(4):
            for kind in range(3):
                for k in range(0, 16, 2):
                    unit(g_qkv, 3 * j + kind, wq, k * 128, k, 2, kind * 2048 + 512 * j, 512, k == 0, k == 14)
        for cs in ((0, 1), (2, 3)):
            for lo, hi in ((0, 12), (12, 16)):
                for c in cs:
                    for k in range(lo, hi, 2):
                        unit(g_wo, c, wo, k * 128, k, 2, 512 * c, 512, k == 0, k == 14)
        g_wo.last_unit = plan[-1]
        g_wo.fence = lambda: spawn(xprep(g_m1, col["norm_mlp_g"], None))

        def m1_units(e):
            for c in range(2):
                for k in range(0, 16, 2):
                    unit(g_m1, 2 * e + c, A["mlp_w_in"][0], k * 128, k, 2, (2 * e + c) * 512, 512, k == 0, k == 14)

        def m2_units(e):
            for c in range(4):
                for k in range(0, 8, 2):
                    unit(m2[e], c, A["mlp_w_out"][0], e * 1024 + k * 128, k, 2, 512 * c, 512, k == 0, k == 6)

        m1_units(0)
        for e in range(1, 8):
            m1_units(e)
            m2_units(e - 1)
        m2_units(7)
        first_end = len(plan)
        m2[7].last_unit = plan[-1]
        start0, go0 = layer(0)
        start1, go1 = layer(1)
        m2[7].fence = lambda: spawn(start0())
        go0.fence = lambda: spawn(start1())

        adas = [(l, pc, kt) for l in range(2) for pc in range(6) for kt in range(16)]
        for i, u in enumerate(plan):
            items.append(("w", u))
            if 8 <= i < first_end and i % 2 == 1 and adas:
                items.append(("a", adas.pop(0)))
            if i == first_end - 8:
                items += [("a", a) for a in adas]
                adas = []
        for _ in range(NR):
            issue_dma()
        spawn(xprep(g_qkv, col["norm_mix_g"], None, vc_tok))
        run()
        SP.ops.append(lambda e: e.wait_ge(s_out, 64))

        block = ctx.enter_context(nc.Block())

        @block.sync
        def _(e):
            for f in SP.ops:
                f(e)

        @block.scalar
        def _(e):
            for f in SC.ops:
                f(e)

        @block.vector
        def _(e):
            for f in VE.ops:
                f(e)

        @block.gpsimd
        def _(e):
            for f in PO.ops:
                f(e)

        @block.tensor
        def _(e):
            for f in PE.ops:
                f(e)


def constants():
    c = np.zeros((128, 6 * 128 + 33), np.float32)
    p, f = np.arange(128)[:, None], np.arange(128)[None, :]
    c[:, 0:128] = p == f
    c[:, 128:256] = p < f
    c[:, 256:384] = -(p > f).astype(np.float32)
    c[:, 384:512] = -1.0
    c[:, 512:640] = np.where(f <= p, 0.0, -1e30)
    c[:, 640:768] = 1.0
    e = np.arange(0, 64, 2, dtype=np.float32) / np.float32(64)
    c[:, 768:800] = np.float32(1.0) / np.power(np.float32(10000.0), e)
    c[:, 800] = -0.5
    return c


_INS = ["x", "norm_mix_g", "norm_mlp_g", "sb_w_qkv", "sb_q_norm_g", "sb_k_norm_g", "sb_w_o", "mlp_w_in", "mlp_w_out",
        "c_2", "positions_2", "ada_w_2", "ada_b_2", "norm_g_2", "w_in_2", "q_lat_g_2", "w_q_up_2", "kv_lat_g_2",
        "w_kv_up_2", "q_norm_g_2", "k_norm_g_2", "glu_b_2", "dw_w_2", "dw_b_2", "conv_ln_g_2", "conv_ln_b_2",
        "w_pw_2", "b_pw_2", "w_out_2"]


def kernel(**inputs):
    import concourse.bacc as _bacc
    from concourse.bass_utils import run_bass_kernel_spmd as _run

    nc = _bacc.Bacc("TRN2", target_bir_lowering=False, num_devices=1)
    arrays, args = {}, {}
    given = {name: np.ascontiguousarray(inputs[name]) for name in _INS}
    given["consts"] = constants()
    for name, a in given.items():
        arrays[f"in_{name}_dram"] = a
        args[name] = nc.dram_tensor(f"in_{name}_dram", a.shape, mybir.dt.from_np(a.dtype), kind="ExternalInput").ap()
    out = nc.dram_tensor("out_0_dram", (1, 256, 2048), F32, kind="ExternalOutput").ap()
    build(nc, args, out)
    r = _run(nc, [arrays], core_ids=[0])
    return r.results[0]["out_0_dram"]
```

```python
import numpy as np
import concourse.bass as bass
from concourse import mybir
from contextlib import ExitStack

F32 = mybir.dt.float32
F32R = mybir.dt.float32r
I32 = mybir.dt.int32
ALU = mybir.AluOpType
ACT = mybir.ActivationFunctionType
AXX = mybir.AxisListType.X
K = 1024
EPS = 1e-6
D = 2048
CONVP = 0


class Engine:

    def __init__(self, sem):
        self.sem, self.n, self.seen, self.ops = sem, 0, {}, []

    def wait(self, *tokens):
        for t in tokens:
            if isinstance(t, list):
                self.wait(*t)
            elif t is not None and self.seen.get(t[0], 0) < t[1]:
                self.seen[t[0]] = t[1]
                self.ops.append(lambda e, s=t[0], v=t[1]: e.wait_ge(s, v))

    def do(self, fn, *after, inc=True):
        self.wait(*after)
        if inc:
            self.n += 1
            self.ops.append(lambda e: fn(e).then_inc(self.sem, 1))
            return (self.sem, self.n)
        self.ops.append(fn)
        return None

    def last(self):
        return (self.sem, self.n) if self.n else None


class Slots:

    def __init__(self, n):
        self.n, self.i, self.rel = n, 0, [[] for _ in range(n)]

    def take(self):
        s = self.i % self.n
        self.i += 1
        assert self.rel[s] is not None, "slot still held"
        w, self.rel[s] = self.rel[s], None
        return s, w

    def release(self, s, *tokens):
        self.rel[s] = list(tokens)


def build(nc, A, out):
    ctx = ExitStack()
    with ctx:
        sem = lambda n: ctx.enter_context(nc.semaphore(n))
        PE, SC, VE, PO, SP = (Engine(sem("s_" + n)) for n in ("pe", "act", "dve", "pool", "sp"))
        base = 16512
        at = [base]

        def put(name, shape, dt=F32, off=None):
            size = int(np.prod(shape[1:])) * 4
            if off is None:
                off = at[0]
                at[0] += (size + 31) // 32 * 32
            return nc.alloc_sbuf_tensor_at(name, shape, dt, offset=off)

        NR, NH, LA = 5, 4, 3
        RAW = put("RAW", [128, NR, 1024])
        WH = put("WH", [128, NH, 1024], F32R)
        WL = put("WL", [128, NH, 1024], F32R)
        X = put("X", [128, 2, D])
        oA = at[0]
        AH = put("AH", [128, 16, 256], F32R)
        AL = put("AL", [128, 16, 256], F32R)
        oBH = at[0]
        BH = put("BH", [128, 16, 256], F32R)
        oBL = at[0]
        BL = put("BL", [128, 16, 256], F32R)
        FB = put("FB", [128, 4, 512])
        PB = put("PB", [128, 4, 256])
        CST = put("CST", [128, 6 * 128 + 32 + 1])
        VC = put("VC", [128, 276])
        DW = put("DW", [128, 2, 8, 31])
        MOD = put("MOD", [128, 2, 48])
        TRG = put("TRG", [128, 4, 64])
        CS = put("CS", [128, 2, 2, 32])
        TQ = put("TQ", [128, 4, 2, 32])
        TK = put("TK", [128, 4, 2, 32])
        CC = put("CC", [128, 16])
        ST = put("ST", [128, 96])
        SCL = put("SCL", [128, 16])
        GQ = put("GQ", [128, 4])
        oS = at[0]
        assert oS + 9152 + 44 * K <= 229344, (229344 - oS) / K

        IDN = CST[:, 0:128]
        MS = CST[:, 128:256]
        UN = CST[:, 256:384]
        NG = CST[:, 384:512]
        NM = CST[:, 512:640]
        ONE = CST[:, 640:768]
        INVF = CST[:, 768:800]
        MH = CST[:, 800:801]

        N = put("N", [128, 2, D], off=oS)
        QK = put("QK", [128, 2, 2, 512], off=oS)
        SQ = put("SQ", [128, 1024], off=oS + 8 * K)
        V1 = put("V1", [128, 2, 512], off=oS + 12 * K)
        QT1 = put("QT1", [128, 2, 4, 256], off=oS + 16 * K)
        TL = put("TL", [128, 4, 384], off=oS + 24 * K)
        TA = put("TA", [128, 4, 384], off=oS + 30 * K)
        TN = put("TN", [128, 4, 384], off=oS + 36 * K)
        ACC2 = put("ADA", [128, 2, 1024], off=oS + 44 * K)
        RN = put("RN", [128, 2, 2, 512], off=oS + 16 * K)
        VR = put("VR", [128, 3, 128], off=oS + 24 * K)
        DR = put("DR", [31, 2, 1024], off=oS + 26 * K)
        PI = put("PI", [128, 2], I32, off=oS + 34 * K)
        AG = put("AG", [128, 8, 64], off=oS + 35 * K)
        UT = put("UT", [128, 8, 286], off=oS)
        LNS = put("LNS", [128, 4, 256], off=oS)
        o2 = oS + 9152
        SMG = put("SMG", [128, 2, 1024], off=o2)
        SCG = put("SCG", [128, 2, 1024], off=o2 + 8 * K)
        KLH = put("KLH", [128, 2, 256], F32R, off=o2 + 16 * K)
        KLL = put("KLL", [128, 2, 256], F32R, off=o2 + 18 * K)
        KV = put("KV", [128, 2, 512], off=o2 + 20 * K)
        QN = put("QN", [128, 2, 384], off=o2 + 24 * K)
        QR = put("QR", [128, 4, 64], off=o2 + 27 * K)
        KR2 = put("KR2", [128, 4, 64], off=o2 + 28 * K)
        TT = put("TTr", [128, 4, 512], off=o2 + 29 * K)
        SCO = put("SCO", [128, 2, 384], off=o2 + 37 * K)
        PTB = put("PTB", [128, 2, 384], off=o2 + 40 * K)
        KR = put("KR", [128, 2, 64], off=o2 + 43 * K)
        RK = put("RK", [128, 2, 64], off=o2 + 43 * K + 512)
        ULH = put("ULH", [128, 8, 256], F32R, off=oA)
        ULL = put("ULL", [128, 8, 256], F32R, off=oA + 8 * K)
        G = put("G", [128, D], off=oA + 16 * K)
        MP = put("MP", [128, 2, 512], off=oA + 24 * K)
        BR = put("BR", [1, 1024], off=oA + 28 * K)
        UV = put("UV", [128, 2, 512], off=oBH)
        UG = put("UG", [128, 2, 512], off=oBH + 4 * K)
        CA = put("CA", [128, 8, 256], off=oBH + 8 * K)
        NQ = put("NQ", [128, 2, 512], off=oBL)
        NK = put("NK", [128, 2, 256], off=oBL + 4 * K)
        QLH = put("QLH", [128, 4, 256], F32R, off=oBL + 8 * K)
        QLL = put("QLL", [128, 4, 256], F32R, off=oBL + 12 * K)

        P = ctx.enter_context(nc.psum_tensor("P", [128, 8, 512], F32))

        f_slots = Slots(4)
        t_slots = Slots(4)
        p_slots = Slots(4)
        pairs = Slots(2)

        def bank():
            s, w = t_slots.take()
            return s, P[:, 4 + s, :], w

        def copy_act(o, i, *w):
            return SC.do(lambda e: e.activation(o, i, ACT.Copy), *w)

        def copy_dve(o, i, *w):
            return VE.do(lambda e: e.tensor_copy(o, i), *w)

        def act(o, i, f, *w, **k):
            return SC.do(lambda e: e.activation(o, i, f, **k), *w)

        def tt(E, o, a, b, op, *w):
            return E.do(lambda e: e.tensor_tensor(o, a, b, op), *w)

        def ts(E, o, a, s1, s2, op0, op1, *w):
            if s2 is None:
                return E.do(lambda e: e.tensor_scalar(o, a, s1, None, op0), *w)
            return E.do(lambda e: e.tensor_scalar(o, a, s1, s2, op0, op1), *w)

        def stt(o, a, s, b, op0, op1, *w):
            return VE.do(lambda e: e.scalar_tensor_tensor(out=o, in0=a, scalar=s, in1=b, op0=op0, op1=op1), *w)

        def red(o, a, op, *w):
            return VE.do(lambda e: e.tensor_reduce(o, a, AXX, op), *w)

        def mm(o, l, r, st, sp, *w, inc=False, **k):
            return PE.do(lambda e: e.matmul(o, l, r, start=st, stop=sp, **k), *w, inc=inc)

        def tr(o, i, ident, *w, inc=False):
            return PE.do(lambda e: e.transpose(o, i, ident), *w, inc=inc)

        def power(o, ms, n, *w):
            return tt(PO, o, ms, MH.to_broadcast([128, n]), ALU.pow, *w)

        def split(f, fs, tok, H, L, *w):
            th = copy_act(H, f, tok, *w)
            tl = tt(VE, L, f, H.bitcast(F32), ALU.subtract, th, tok, *w)
            f_slots.release(fs, tl)
            return tl

        def flip(src, kts, wsrc, done, H, L, evac, *w):
            b, pb, wb = bank()
            for i, kt in enumerate(kts):
                for t in range(2):
                    last = tr(pb[:, (2 * i + t) * 128:(2 * i + t + 1) * 128], src(kt, t), IDN, wb, wsrc, c_tok,
                              inc=(i == 1 and t == 1))
            fs, wf = f_slots.take()
            f = FB[:, fs, :]
            te = evac(f, pb, kts, [last, wf])
            t_slots.release(b, te)
            tl = split(f, fs, te, H, L, *w)
            for kt in kts:
                done[kt] = tl
            return last, tl

        def affine(s, b, E):
            def go(f, pb, kts, w):
                for i, kt in enumerate(kts):
                    o, q = f[:, i * 256:(i + 1) * 256], pb[:, i * 256:(i + 1) * 256]
                    if E is SC and b is None:
                        te = act(o, q, ACT.Copy, w, scale=s[:, kt:kt + 1])
                    elif E is SC:
                        te = act(o, q, ACT.Identity, w, scale=s[:, kt:kt + 1], bias=b[:, kt:kt + 1])
                    elif b is None:
                        te = ts(VE, o, q, s[:, kt:kt + 1], None, ALU.mult, None, w)
                    else:
                        te = ts(VE, o, q, s[:, kt:kt + 1], b[:, kt:kt + 1], ALU.mult, ALU.add, w)
                return te
            return go

        def plain(f, pb, kts, w):
            return copy_act(f, pb, w)

        def squared(f, pb, kts, w):
            return act(f, pb, ACT.Square, w)

        s_c, s_v, s_g, s_br = sem("s_c"), sem("s_v"), sem("s_g"), sem("s_br")
        s_x = [sem(f"s_x{c}") for c in range(4)]
        c_tok = (s_c, 16)
        x_in = A["x"][0].rearrange("(t p) d -> p t d", p=128)

        def load_x(c):
            SP.ops.append(lambda e: e.dma_start(X[:, :, c * 512:(c + 1) * 512], x_in[:, :, c * 512:(c + 1) * 512]).then_inc(s_x[c], 16))

        SC.ops.append(lambda e: e.dma_start(VR[0:16, 0, :], A["norm_mix_g"].rearrange("a (r p) -> (a r) p", p=128)).then_inc(s_g, 16))
        SC.ops.append(lambda e: e.dma_start(CST[:, :], A["consts"]).then_inc(s_c, 16))
        for c in range(4):
            load_x(c)
        rows = [[("norm_mlp_g", 16), ("norm_g_2", 32), ("q_lat_g_2", 8), ("kv_lat_g_2", 4),
                 ("conv_ln_g_2", 16), ("conv_ln_b_2", 16), ("sb_q_norm_g", 1), ("sb_k_norm_g", 1),
                 ("q_norm_g_2", 2), ("k_norm_g_2", 2)],
                [("dw_b_2", 16), ("glu_b_2", 32), ("c_2", 16)], [("ada_b_2", 96)]]
        col, nrow, vload, at_col = {"norm_mix_g": VC[:, 0:16]}, [16, 0, 0], [], [0, 114, 178]
        for g, names in enumerate(rows):
            for name, n in names:
                r = nrow[g]
                src = A[name][:, 0:128] if name in ("q_norm_g_2", "k_norm_g_2") else A[name].rearrange("a (r p) -> (a r) p", p=128)
                vload.append((VR[r:r + n, g, :], src, {}))
                col[name] = VC[:, at_col[g] + r:at_col[g] + r + n]
                nrow[g] = r + n
        assert nrow == [114, 64, 96]
        vload.append((DR[:, :, :], A["dw_w_2"].rearrange("l k c -> k l c"), {}))
        vload.append((PI[:, :], A["positions_2"].rearrange("a (t p) -> p (a t)", p=128), {"allow_slow_non_contiguous": True}))
        for l in range(2):
            vload.append((TRG[:, 2 * l, :], A["q_norm_g_2"][l:l + 1, 128:192].to_broadcast([128, 64]), {}))
            vload.append((TRG[:, 2 * l + 1, :], A["k_norm_g_2"][l:l + 1, 128:192].to_broadcast([128, 64]), {}))
        v_tok = (s_v, 16 * len(vload))

        b, pb, wb = bank()
        last = tr(pb[:, 0:16], VR[0:16, 0, :], CST[0:16, 0:16], (s_g, 16), c_tok, inc=True)
        mg_tok = copy_dve(VC[:, 0:16], pb[:, 0:16], last)
        t_slots.release(b, mg_tok)
        C = {}

        def load_vectors():
            for dst, src, k in vload:
                SC.ops.append(lambda e, dst=dst, src=src, k=k: e.dma_start(dst, src, **k).then_inc(s_v, 16))
            SC.ops.append(lambda e: e.preload_act_table_set("silu_and_others"))
            yield
            yield
            yield
            yield
            b, pb, wb = bank()
            for g in range(3):
                n = nrow[g]
                last = tr(pb[:, g * 128:g * 128 + n], VR[0:n, g, :], CST[0:n, 0:n], v_tok, c_tok, wb, inc=(g == 2))
            copy_dve(VC[:, 16:114], pb[:, 16:114], last)
            copy_dve(VC[:, 114:178], pb[:, 128:192], last)
            C["vc"] = vc_tok = copy_dve(VC[:, 178:274], pb[:, 256:352], last)
            t_slots.release(b, vc_tok)
            C["cc"] = act(CC[:, :], col["c_2"], ACT.Silu, vc_tok)
            ts(VE, GQ[:, 0:1], col["sb_q_norm_g"], 128.0 ** -0.5, None, ALU.mult, None, vc_tok)
            C["gq"] = tt(VE, GQ[:, 1:3], col["q_norm_g_2"], col["k_norm_g_2"], ALU.mult, vc_tok)
            b, pb, wb = bank()
            for l in range(2):
                for c in range(8):
                    o = (l * 8 + c) * 31
                    last = tr(pb[:, o:o + 31], DR[0:31, l, c * 128:(c + 1) * 128], CST[0:31, 0:31], wb, v_tok, inc=(l == 1 and c == 7))
            C["dw"] = copy_dve(DW[:, :, :, :].rearrange("p a b c -> p (a b c)"), pb[:, 0:496], last)
            t_slots.release(b, C["dw"])
            yield
            posf, ang, kk = AG[:, 0, 0:2], AG[:, 1, :], AG[:, 2, :]
            t0 = copy_dve(posf, PI[:, :], v_tok)
            for t in range(2):
                t1 = ts(VE, ang[:, 32 * t:32 * t + 32], INVF, posf[:, t:t + 1], None, ALU.mult, None, t0, c_tok)
            t1 = ts(VE, kk, ang, float(np.float32(1 / (2 * np.pi))), None, ALU.mult, None, t1)
            t1 = ts(VE, kk, kk, 12582912.0, None, ALU.add, None, t1)
            t1 = ts(VE, kk, kk, -12582912.0, None, ALU.add, None, t1)
            r1, cur = 2 * np.pi, ang
            for i in range(3):
                part = np.float32(r1)
                if i < 2:
                    part = np.uint32(part.view(np.uint32) & np.uint32(0xFFFF8000)).view(np.float32)
                r1 -= float(part)
                t1 = stt(AG[:, 3 + i, :], kk, -float(part), cur, ALU.mult, ALU.add, t1)
                cur = AG[:, 3 + i, :]
            t1 = ts(VE, cur, cur, float(np.float32(3.1415925)), float(np.float32(-3.1415925)), ALU.min, ALU.max, t1)
            sv = CS[:, 1, :, :].rearrange("p t f -> p (t f)")
            cv = CS[:, 0, :, :].rearrange("p t f -> p (t f)")
            act(sv, cur, ACT.Sin, t1)
            t2 = ts(VE, AG[:, 6, :], cur, -1.0, None, ALU.mult, None, t1)
            t2 = tt(VE, AG[:, 7, :], cur, AG[:, 6, :], ALU.max, t2)
            t2 = ts(VE, AG[:, 6, :], AG[:, 7, :], -1.0, float(np.float32(np.pi / 2)), ALU.mult, ALU.add, t2)
            C["cs"] = act(cv, AG[:, 6, :], ACT.Sin, t2)
            SC.ops.append(lambda e: e.preload_act_table_set("natural_log_exp_and_others"))

        class Gemm:
            def __init__(self, H, L, done):
                self.H, self.L, self.done, self.tok, self.bias, self.fence = H, L, done, {}, None, None
                self.end, self.last_unit, self.pair = None, None, {}

        plan = []

        def unit(g, c, src, r0, k0, nk, c0, w, st, sp):
            plan.append(dict(g=g, c=c, src=src, r0=r0, k0=k0, nk=nk, c0=c0, w=w, st=st, sp=sp))

        jobs = []

        def spawn(gen):
            jobs.append(gen)

        def pump():
            for j in list(jobs):
                try:
                    next(j)
                except StopIteration:
                    jobs.remove(j)

        raw_sem = [sem(f"s_raw{i}") for i in range(NR)]
        items, raw_free, state = [], {}, dict(dma=0, item=0)
        hl_slots = Slots(NH)
        wtok = {}

        def issue_dma():
            i = state["dma"]
            if i >= len(items):
                return
            state["dma"] += 1
            kind, u = items[i]
            s = i % NR
            SP.wait(raw_free.get(i - NR))
            if kind == "w":
                dst = RAW[:, s, 0:u["nk"] * u["w"]].rearrange("p (k n) -> p k n", k=u["nk"])
                src = u["src"][u["r0"]:u["r0"] + 128 * u["nk"], u["c0"]:u["c0"] + u["w"]].rearrange("(k p) n -> p k n", p=128)
            else:
                l, pc, kt = u
                dst = RAW[:, s, :]
                src = A["ada_w_2"][l, kt * 128:(kt + 1) * 128, pc * 1024:(pc + 1) * 1024]
            SP.ops.append(lambda e: e.dma_start(dst, src).then_inc(raw_sem[s], 16))

        ada_slots = Slots(2)
        ada = dict(tok=None, slot=0, w=None)
        mod_tok = {}

        def ada_reduce(l, pc, slot, tok):
            b, pb, wb = bank()
            for j in range(8):
                last = mm(pb[:, j:j + 1], ACC2[:, slot, j * 128:(j + 1) * 128], ONE[:, 0:1], True, True, wb, tok, c_tok, inc=(j == 7))
            ada_slots.release(slot, last)
            o = 8 * pc
            te = tt(VE, MOD[:, l, o:o + 8], pb[:, 0:8], col["ada_b_2"][:, 48 * l + o:48 * l + o + 8], ALU.add, last, C["vc"])
            t_slots.release(b, te)
            mod_tok[l] = te
            yield

        def take_item():
            i = state["item"]
            state["item"] += 1
            kind, u = items[i]
            s = i % NR
            there = (raw_sem[s], 16 * (i // NR + 1))
            if kind == "a":
                l, pc, kt = u
                if kt == 0:
                    ada["slot"], ada["w"] = ada_slots.take()
                acc = ACC2[:, ada["slot"], :]
                sc = CC[:, kt:kt + 1]
                if kt == 0:
                    t = ts(VE, acc, RAW[:, s, :], sc, None, ALU.mult, None, there, ada["w"], C["cc"])
                else:
                    t = stt(acc, RAW[:, s, :], sc, acc, ALU.mult, ALU.add, there, ada["tok"])
                ada["tok"] = t
                raw_free[i] = t
                if kt == 15:
                    spawn(ada_reduce(l, pc, ada["slot"], t))
            else:
                n = u["nk"] * u["w"]
                h, wh = hl_slots.take()
                r, H, L = RAW[:, s, 0:n], WH[:, h, 0:n], WL[:, h, 0:n]
                th = copy_act(H, r, there, wh)
                tl = tt(VE, L, r, H.bitcast(F32), ALU.subtract, there, th)
                raw_free[i] = tl
                wtok[id(u)] = (h, tl, th)
            issue_dma()
            return kind

        def run():
            w_at = [0]

            def prefetch(to):
                while w_at[0] < min(to, len(plan)):
                    if take_item() == "w":
                        w_at[0] += 1

            for i, u in enumerate(plan):
                prefetch(i + 1 + LA)
                g = u["g"]
                for k in range(u["nk"]):
                    while u["k0"] + k not in g.tok:
                        assert jobs
                        pump()
                if u["st"]:
                    while pairs.rel[pairs.i % 2] is None:
                        pump()
                    p, wp = pairs.take()
                    g.pair[u["c"]] = p
                    PE.wait(wp)
                p = g.pair[u["c"]]
                st = u["st"]
                if st and g.bias:
                    for t in range(2):
                        g.bias(P[:, 2 * p + t, 0:u["w"]], u["c"])
                    st = False
                h, tl, th = wtok[id(u)]
                W = u["w"]
                PE.wait(th, tl)
                for k in range(u["nk"]):
                    kt = u["k0"] + k
                    PE.wait(g.tok[kt])
                    wh, wl = WH[:, h, k * W:(k + 1) * W], WL[:, h, k * W:(k + 1) * W]
                    for t in range(2):
                        o = P[:, 2 * p + t, 0:W]
                        xh, xl = g.H[:, kt, t * 128:(t + 1) * 128], g.L[:, kt, t * 128:(t + 1) * 128]
                        end = k == u["nk"] - 1
                        mm(o, xh, wh, st and k == 0, False)
                        mm(o, xh, wl, False, False)
                        last = mm(o, xl, wh, False, u["sp"] and end, inc=(end and t == 1))
                hl_slots.release(h, last)
                g.end = last
                if u["sp"]:
                    spawn(g.done(u["c"], p, last))
                pump()
                if g.fence and i + 1 < len(plan) and u is g.last_unit:
                    g.fence()
            while jobs:
                pump()

        xs = {(c, t): (s_x[c], 16) for c in range(4) for t in range(2)}
        rms = {}

        def x_square(c):
            for t in range(2):
                fs, wf = f_slots.take()
                q = act(FB[:, fs, :], X[:, t, c * 512:(c + 1) * 512], ACT.Square, xs[(c, t)], wf, rms.get("used"),
                        accum_out=ST[:, 64 + 4 * t + c:65 + 4 * t + c])
                f_slots.release(fs, q)
            rms[c] = q
            if all(i in rms for i in range(4)):
                q = red(ST[:, 72:74], ST[:, 64:72].rearrange("p (a b) -> p a b", b=4), ALU.add, [rms.pop(i) for i in range(4)])
                q = ts(VE, ST[:, 72:74], ST[:, 72:74], 1.0 / D, EPS, ALU.mult, ALU.add, q)
                rms["tok"] = power(ST[:, 74:76], ST[:, 72:74], 2, q, c_tok, rms.get("read"))

        def x_flip(dst, gain, c, *w):
            for k in (4 * c, 4 * c + 2):
                last, tl = flip(lambda kt, tk: X[:, tk, kt * 128:(kt + 1) * 128], (k, k + 1), [xs[(c, 0)], xs[(c, 1)]], dst.tok,
                                dst.H[:, k:k + 2, :].rearrange("p a b -> p (a b)"), dst.L[:, k:k + 2, :].rearrange("p a b -> p (a b)"),
                                affine(gain, None, VE), *w)
                rms["fliptok"] = last
                yield

        def x_start():
            VE.wait(mg_tok)
            for c in range(4):
                for _ in x_flip(g_qkv, col["norm_mix_g"], c, mg_tok):
                    pass
            for c in range(4):
                x_square(c)
            yield

        def xprep(dst, scale, bias, *w):
            t = rms["tok"]
            nt = {}
            for j in range(4):
                for tk in range(2):
                    nt[j] = ts(VE, N[:, tk, j * 512:(j + 1) * 512], X[:, tk, j * 512:(j + 1) * 512], ST[:, 74 + tk:75 + tk], None,
                               ALU.mult, None, t, xs[(j, tk)], *w)
                for k in (4 * j, 4 * j + 2):
                    last, tl = flip(lambda kt, tk: N[:, tk, kt * 128:(kt + 1) * 128], (k, k + 1), nt[j], dst.tok,
                                    dst.H[:, k:k + 2, :].rearrange("p a b -> p (a b)"), dst.L[:, k:k + 2, :].rearrange("p a b -> p (a b)"),
                                    affine(scale, bias, SC), *w)
            rms["used"] = rms["read"] = nt[3]
            rms["n"] = last
            yield

        qkt = dict(nat=[None, None], T=[None, None], rT=[None, None], V=None, rV=None)
        wo_tok = {}

        def qkv_done(c, p, tok):
            j, kind = c // 3, c % 3
            if kind == 2:
                for t in range(2):
                    te = act(V1[:, t, :], P[:, 2 * p + t, :], ACT.Copy, tok, qkt["rV"], rms["tok"], scale=ST[:, 74 + t:75 + t])
                pairs.release(p, te)
                qkt["V"] = te
                spawn(sb_heads(j, 0))
                spawn(sb_heads(j, 1))
                return
            nat = QK[:, kind, :, :].rearrange("p t n -> p (t n)")
            for t in range(2):
                te = act(QK[:, kind, t, :], P[:, 2 * p + t, :], ACT.Copy, tok, qkt["nat"][kind], rms["tok"], scale=ST[:, 74 + t:75 + t])
            rms["read"] = te
            pairs.release(p, te)
            n8 = nat.rearrange("p (a d) -> p a d", d=128)
            q = tt(PO, SQ[:, :], nat, nat, ALU.mult, te)
            o = 8 + 24 * kind
            q = red(ST[:, o:o + 8], SQ[:, :].rearrange("p (a d) -> p a d", d=128), ALU.add, q)
            q = ts(VE, ST[:, o + 8:o + 16], ST[:, o:o + 8], 1.0 / 128, EPS, ALU.mult, ALU.add, q)
            yield
            q = power(ST[:, o + 16:o + 24], ST[:, o + 8:o + 16], 8, q)
            q = tt(PO, n8, n8, ST[:, o + 16:o + 24].rearrange("p (a b) -> p a b", b=1).to_broadcast([128, 8, 128]), ALU.mult, q)
            yield
            sc = GQ[:, 0:1] if kind == 0 else col["sb_k_norm_g"]
            for hp in range(2):
                b, pb, wb = bank()
                for h in range(2):
                    for t in range(2):
                        last = tr(pb[:, (2 * h + t) * 128:(2 * h + t + 1) * 128], QK[:, kind, t, (2 * hp + h) * 128:(2 * hp + h + 1) * 128],
                                  IDN, wb, q, inc=(h == 1 and t == 1))
                te = act(QT1[:, kind, 2 * hp:2 * hp + 2, :].rearrange("p a b -> p (a b)"), pb, ACT.Copy, last, C["gq"], C["vc"],
                         qkt["rT"][kind], scale=sc)
                t_slots.release(b, te)
            qkt["nat"][kind] = last
            qkt["T"][kind] = te

        tl_rel = [None, None]

        def sb_heads(j, hp):
            while None in qkt["T"]:
                yield
            sl, t1s, nls = [], [], []
            for i in range(2):
                h, s = 2 * hp + i, 2 * hp + i
                b, pb, wb = bank()
                mm(pb[:, 0:256], QT1[:, 1, h, 0:128], QT1[:, 0, h, :], True, True, wb, qkt["T"])
                last = mm(pb[:, 256:384], QT1[:, 1, h, 128:256], QT1[:, 0, h, 128:256], True, True, inc=True)
                z = pb[:, 0:384]
                t = act(TL[:, s, :], z, ACT.Abs, last, tl_rel[hp])
                t = act(TL[:, s, :], TL[:, s, :], ACT.Exp, t, scale=-1.0)
                t = act(TL[:, s, :], TL[:, s, :], ACT.Ln, t, bias=1.0)
                t1 = stt(TA[:, s, :], z, 0.0, TL[:, s, :], ALU.min, ALU.subtract, t, tl_rel[hp])
                t2 = stt(TN[:, s, :], z, 0.0, TL[:, s, :], ALU.max, ALU.add, t, tl_rel[hp])
                t_slots.release(b, t2)
                nd = TN[:, s, :].rearrange("p (a b) -> p a b", b=128)[:, 0:3:2, :]
                t3 = tt(PO, nd, nd, MS.rearrange("p (a b) -> p a b", a=1).to_broadcast([128, 2, 128]), ALU.mult, t2)
                t1s.append(t1)
                nls.append(t3)
            qkt["rT"] = [last, last]
            yield
            as_ = []
            for i in range(2):
                s = 2 * hp + i
                b, pb, wb = bank()
                mm(pb[:, 0:128], UN, TN[:, s, 0:128], True, True, wb, nls[i])
                mm(pb[:, 128:256], UN, TN[:, s, 128:256], True, False)
                mm(pb[:, 128:256], NG, TN[:, s, 256:384], False, True)
                last = mm(pb[:, 256:384], UN, TN[:, s, 256:384], True, True, inc=True)
                t = tt(VE, TA[:, s, :], pb[:, 0:384], TA[:, s, :], ALU.add, last, t1s[i])
                t_slots.release(b, t)
                t = act(TA[:, s, :], TA[:, s, :], ACT.Exp, t)
                ad = TA[:, s, :].rearrange("p (a b) -> p a b", b=128)[:, 0:3:2, :]
                as_.append(tt(PO, ad, ad, MS.rearrange("p (a b) -> p a b", a=1).to_broadcast([128, 2, 128]), ALU.mult, t))
            yield
            b, pb, wb = bank()
            for i in range(2):
                h, s = 2 * hp + i, 2 * hp + i
                o = pb[:, i * 256:(i + 1) * 256]
                v0, v1 = V1[:, 0, h * 128:(h + 1) * 128], V1[:, 1, h * 128:(h + 1) * 128]
                mm(o[:, 0:128], v0, TA[:, s, 0:128], True, True, wb, as_[i], qkt["V"])
                mm(o[:, 128:256], v0, TA[:, s, 128:256], True, False)
                last = mm(o[:, 128:256], v1, TA[:, s, 256:384], False, True, inc=(i == 1))
            tl_rel[hp] = last
            qkt["rV"] = last
            fs, wf = f_slots.take()
            te = copy_act(FB[:, fs, :], pb, last, wf)
            t_slots.release(b, te)
            kt = 4 * j + 2 * hp
            tl = split(FB[:, fs, :], fs, te, BH[:, kt:kt + 2, :].rearrange("p a b -> p (a b)"), BL[:, kt:kt + 2, :].rearrange("p a b -> p (a b)"))
            g_wo.tok[kt] = g_wo.tok[kt + 1] = tl

        def add_x(c, p, tok):
            for t in range(2):
                o = X[:, t, c * 512:(c + 1) * 512]
                te = tt(VE, o, o, P[:, 2 * p + t, :], ALU.add, tok, xs[(c, t)], rms.get("fliptok"))
                xs[(c, t)] = te
            pairs.release(p, te)
            return
            yield

        def wo_done(c, p, tok):
            yield from add_x(c, p, tok)
            x_square(c)
            VE.wait(C["vc"])
            yield from x_flip(g_m1, col["norm_mlp_g"], c, g_qkv.end)

        def last_m2_done(c, p, tok):
            yield from add_x(c, p, tok)
            x_square(c)

        g_qkv = Gemm(AH, AL, qkv_done)
        g_wo = Gemm(BH, BL, wo_done)

        g_m1 = Gemm(AH, AL, None)
        rn_slots = Slots(2)
        m2 = [Gemm(BH[:, 8 * (e % 2):8 * (e % 2) + 8, :], BL[:, 8 * (e % 2):8 * (e % 2) + 8, :], add_x if e < 7 else last_m2_done) for e in range(8)]

        def m1_done(c, p, tok):
            e, cc = c // 2, c % 2
            s, ws = rn_slots.take()
            for t in range(2):
                te = act(RN[:, s, t, :], P[:, 2 * p + t, :], ACT.Relu, tok, ws, rms["tok"], scale=ST[:, 74 + t:75 + t])
            rms["read"] = te
            pairs.release(p, te)
            free = m2[e - 2].end if e >= 2 else g_wo.end
            yield
            for i in (0, 2):
                k = 4 * cc + i
                last, tl = flip(lambda kt, t: RN[:, s, t, (kt - 4 * cc) * 128:(kt - 4 * cc + 1) * 128], (k, k + 1), te, m2[e].tok,
                                m2[e].H[:, k:k + 2, :].rearrange("p a b -> p (a b)"), m2[e].L[:, k:k + 2, :].rearrange("p a b -> p (a b)"),
                                squared, free)
                if i == 2:
                    rn_slots.release(s, last)
                yield

        g_m1.done = m1_done

        def layer(l):
            gz = Gemm(AH, AL, None)
            gq = Gemm(QLH, QLL, None)
            gk = Gemm(KLH, KLL, None)
            gp = Gemm(ULH, ULL, None)
            go = Gemm(BH, BL, None)
            T = {}
            cgl = lambda name, n: col[name][:, n * l:n * l + n]

            def start():
                t = stt(SCL[:, :], MOD[:, l, 16:32], 1.0, cgl("norm_g_2", 16), ALU.add, ALU.mult, mod_tok[l], C["vc"], scl.get("r"))
                SC.wait(t, C["vc"])
                yield from xprep(gz, SCL, MOD[:, l, 0:16], gz_free[l]())
                T["pad"] = VE.do(lambda e: e.memset(UT[:, :, 0:30], 0.0), rms["n"])
                for tab, gi in ((TQ, 2 * l), (TK, 2 * l + 1)):
                    for i, (gs, f) in enumerate(((0, 0), (32, 1), (32, 0), (0, 1))):
                        T["tab"] = tt(PO, tab[:, i, :, :], CS[:, f, :, :],
                                      TRG[:, gi:gi + 1, gs:gs + 32].to_broadcast([128, 2, 32]), ALU.mult, C["cs"], v_tok)

            uv = {}
            conv = {}

            def z_done(c, p, tok):
                pp = [P[:, 2 * p, :], P[:, 2 * p + 1, :]]
                if c in (0, 2):
                    for t in range(2):
                        te = copy_act(UV[:, t, :], pp[t], tok, T.get("uvr"))
                    pairs.release(p, te)
                    T["uv"] = te
                    return
                if c in (1, 3):
                    j = c // 2
                    for t in range(2):
                        te = copy_act(UG[:, t, :], pp[t], tok, T.get("uvr"))
                    pairs.release(p, te)
                    bg = cgl("glu_b_2", 16)
                    yield
                    for i in range(4):
                        ct = 4 * j + i
                        b, pb, wb = bank()
                        for t in range(2):
                            tr(pb[:, t * 128:(t + 1) * 128], UV[:, t, i * 128:(i + 1) * 128], IDN, wb, te, T["uv"])
                            last = tr(pb[:, 256 + t * 128:256 + (t + 1) * 128], UG[:, t, i * 128:(i + 1) * 128], IDN, inc=(t == 1))
                        fs, wf = f_slots.take()
                        ta = act(FB[:, fs, 0:256], pb[:, 256:512], ACT.Sigmoid, last, wf, bias=bg[:, 8 + ct:9 + ct])
                        tb = stt(UT[:, ct, 30:286], pb[:, 0:256], bg[:, ct:ct + 1], FB[:, fs, 0:256], ALU.add, ALU.mult, ta, T["pad"])
                        f_slots.release(fs, tb)
                        t_slots.release(b, tb)
                        conv[ct] = tb
                        if i % 2:
                            yield
                    T["uvr"] = last
                    spawn(convolve(range(4 * j, 4 * j + 4), (3, 6, 7)))
                    return
                if c == 4:
                    for t in range(2):
                        te = copy_act(NQ[:, t, :], pp[t], tok)
                    pairs.release(p, te)
                    yield from latent(NQ, 512, te, 6, gq, QLH, QLL, cgl("q_lat_g_2", 4))
                    return
                if c == 5:
                    for t in range(2):
                        te = copy_act(NK[:, t, :], pp[t][:, 0:256], tok)
                        te = copy_act(KR[:, t, :], pp[t][:, 256:320], tok)
                    pairs.release(p, te)
                    q = tt(PO, FBk, KR[:, :, :], KR[:, :, :], ALU.mult, te)
                    T["ssr"] = red(ST[:, 56:58], FBk, ALU.add, q)
                    q = te
                    for t in range(2):
                        q = rope(RK[:, t:t + 1, :], KR[:, t:t + 1, :], TK, t, [1], q)
                    T["rk"] = q
                    yield from latent(NK, 256, te, 14, gk, KLH, KLL, cgl("kv_lat_g_2", 2))
                    return
                dst = SMG if c < 8 else SCG
                o = (c % 2) * 512
                for t in range(2):
                    te = act(dst[:, t, o:o + 512], pp[t], ACT.Silu, tok)
                pairs.release(p, te)
                T["g", c] = te

            FBk = UTk[:, :].rearrange("p (a b) -> p a b", a=2)

            def rope(o, x, tab, t, shape, *w):
                n = shape[0]
                tb = [tab[:, i, t:t + 1, :].to_broadcast([128, n, 32]) for i in range(4)]
                tm = RT[:, 0:4 * n * 32].rearrange("p (i a b) -> p i a b", i=4, a=n)
                x1, x2 = x[:, :, 0:32], x[:, :, 32:64]
                q0 = tt(PO, tm[:, 0, :, :], x1, tb[0], ALU.mult, T["tab"], *w)
                q1 = tt(PO, tm[:, 1, :, :], x2, tb[1], ALU.mult)
                q2 = tt(PO, tm[:, 2, :, :], x2, tb[2], ALU.mult)
                q3 = tt(PO, tm[:, 3, :, :], x1, tb[3], ALU.mult)
                q = tt(PO, o[:, :, 0:32], tm[:, 0, :, :], tm[:, 1, :, :], ALU.subtract, q1)
                return tt(PO, o[:, :, 32:64], tm[:, 2, :, :], tm[:, 3, :, :], ALU.add, q3)

            def latent(NAT, n, te, o, g, H, L, gain):
                for t in range(2):
                    fs, wf = f_slots.take()
                    q = act(FB[:, fs, 0:n], NAT[:, t, :], ACT.Square, te, wf, accum_out=ST[:, o + t:o + t + 1])
                    f_slots.release(fs, q)
                q = ts(VE, ST[:, o + 2:o + 4], ST[:, o:o + 2], 1.0 / n, EPS, ALU.mult, ALU.add, q)
                q = power(ST[:, o + 4:o + 6], ST[:, o + 2:o + 4], 2, q)
                yield
                for t in range(2):
                    q2 = ts(VE, NAT[:, t, :], NAT[:, t, :], ST[:, o + 4 + t:o + 5 + t], None, ALU.mult, None, q)
                yield
                for k in range(0, n // 128, 2):
                    flip(lambda kt, t: NAT[:, t, kt * 128:(kt + 1) * 128], (k, k + 1), q2, g.tok,
                         H[:, k:k + 2, :].rearrange("p a b -> p (a b)"), L[:, k:k + 2, :].rearrange("p a b -> p (a b)"), affine(gain, None, SC))
                    yield

            def convolve(cts, pool):
                while cts[0] and "conv0" not in T:
                    yield
                ctok = {}
                for k in range(31):
                    for ct in cts:
                        x, w, cb = UT[:, ct, k:k + 256], DW[:, l, ct, k:k + 1], cgl("dw_b_2", 8)[:, ct:ct + 1]
                        if ct in pool and k == 0:
                            ctok[ct] = act(CA[:, ct, :], x, ACT.Identity, conv[ct], C["dw"], scale=w, bias=cb)
                        elif ct in pool:
                            s, wp = p_slots.take()
                            ta = act(PB[:, s, :], x, ACT.Copy, conv[ct], C["dw"], wp, scale=w)
                            ctok[ct] = tt(PO, CA[:, ct, :], CA[:, ct, :], PB[:, s, :], ALU.add, ta, ctok[ct])
                            p_slots.release(s, ctok[ct])
                        elif k == 0:
                            ctok[ct] = ts(VE, CA[:, ct, :], x, w, cb, ALU.mult, ALU.add, conv[ct], C["dw"])
                        else:
                            ctok[ct] = stt(CA[:, ct, :], x, w, CA[:, ct, :], ALU.mult, ALU.add, ctok[ct])
                    yield
                T["conv0" if cts[0] == 0 else "conv1"] = list(ctok.values())
                if cts[0]:
                    T["conv"] = T["conv0"] + T["conv1"]

            def layernorm():
                b, pb, wb = bank()
                for ct in range(8):
                    last = mm(pb[:, 0:256], ONE, CA[:, ct, :], ct == 0, ct == 7, wb, T["conv"], inc=(ct == 7))
                mu = LNS[:, 0, :]
                t = ts(VE, mu, pb[:, 0:256], 1.0 / 1024, None, ALU.mult, None, last)
                t_slots.release(b, t)
                t = tt(VE, CA[:, :, :], CA[:, :, :], LNS[:, 0:1, :].to_broadcast([128, 8, 256]), ALU.subtract, t)
                yield
                b, pb, wb = bank()
                for cp in range(4):
                    fs, wf = f_slots.take()
                    q = act(FB[:, fs, :], CA[:, 2 * cp:2 * cp + 2, :].rearrange("p a b -> p (a b)"), ACT.Square, t, wf)
                    for i in range(2):
                        for tk in range(2):
                            last = mm(pb[:, tk:tk + 1], FB[:, fs, i * 256 + tk * 128:i * 256 + (tk + 1) * 128], ONE[:, 0:1],
                                      cp == 0 and i == 0 and tk == 0, cp == 3 and i == 1 and tk == 1, wb, q,
                                      inc=(i == 1 and tk == 1), skip_group_check=True)
                    f_slots.release(fs, last)
                q = ts(VE, ST[:, 76:78], pb[:, 0:2], 1.0 / 1024, EPS, ALU.mult, ALU.add, last)
                t_slots.release(b, q)
                q = power(ST[:, 78:80], ST[:, 76:78], 2, q)
                yield
                b, pb, wb = bank()
                for t in range(2):
                    last = mm(pb[:, t * 128:(t + 1) * 128], ST[:, 78 + t:79 + t].to_broadcast([128, 128]), IDN, True, True, wb, q, inc=(t == 1))
                q = copy_dve(LNS[:, 2, :], pb[:, 0:256], last)
                t_slots.release(b, q)
                q = tt(VE, CA[:, :, :], CA[:, :, :], LNS[:, 2:3, :].to_broadcast([128, 8, 256]), ALU.mult, q)
                lg, lb = cgl("conv_ln_g_2", 8), cgl("conv_ln_b_2", 8)
                for cp in range(4):
                    fs, wf = f_slots.take()
                    for i in range(2):
                        ct = 2 * cp + i
                        te = act(FB[:, fs, i * 256:(i + 1) * 256], CA[:, ct, :], ACT.Silu, q, wf, scale=lg[:, ct:ct + 1], bias=lb[:, ct:ct + 1])
                    tl = split(FB[:, fs, :], fs, te, ULH[:, 2 * cp:2 * cp + 2, :].rearrange("p a b -> p (a b)"),
                               ULL[:, 2 * cp:2 * cp + 2, :].rearrange("p a b -> p (a b)"), gz.end)
                    gp.tok[2 * cp] = gp.tok[2 * cp + 1] = tl
                    yield

            att = dict(q=[], k=[], free_nat=None, freeT=None, freeKV=None)

            def q_done(g, p, tok):
                while att.get("busyq"):
                    yield
                att["busyq"] = True
                for t in range(2):
                    te = copy_act(QN[:, t, :], P[:, 2 * p + t, 0:384], tok, att.get("rq"))
                pairs.release(p, te)
                for t in range(2):
                    fs, wf = f_slots.take()
                    q = tt(PO, FB[:, fs, 0:384], QN[:, t, :], QN[:, t, :], ALU.mult, te, wf)
                    q = red(ST[:, 20 + 2 * t:22 + 2 * t], FB[:, fs, 0:384].rearrange("p (a d) -> p a d", a=2), ALU.add, q)
                    f_slots.release(fs, q)
                q = ts(VE, ST[:, 24:28], ST[:, 20:24], 1.0 / 192, EPS, ALU.mult, ALU.add, q)
                yield
                q = power(ST[:, 28:32], ST[:, 24:28], 4, q)
                x = QN[:, :, :].rearrange("p t (h d) -> p (t h) d", h=2)
                q = tt(PO, x, x, ST[:, 28:32].rearrange("p (a b) -> p a b", b=1).to_broadcast([128, 4, 192]), ALU.mult, q)
                for t in range(2):
                    q = rope(QR[:, 2 * t:2 * t + 2, :], x[:, 2 * t:2 * t + 2, 128:192], TQ, t, [2], q, att.get("rq"))
                yield
                att["qn"] = q

            def kv_done(g, p, tok):
                while att.get("busyk"):
                    yield
                att["busyk"] = True
                for t in range(2):
                    te = copy_act(KV[:, t, :], P[:, 2 * p + t, :], tok, att.get("rkv"))
                pairs.release(p, te)
                kv = KV[:, :, :].rearrange("p t (h d) -> p (t h) d", h=2)
                kn = kv[:, :, 0:128]
                fs, wf = f_slots.take()
                f4 = FB[:, fs, :].rearrange("p (a d) -> p a d", a=4)
                q = tt(PO, f4, kn, kn, ALU.mult, te, wf)
                q = red(ST[:, 32:36], f4, ALU.add, q)
                f_slots.release(fs, q)
                for t in range(2):
                    q2 = ts(VE, ST[:, 36 + 2 * t:38 + 2 * t], ST[:, 32 + 2 * t:34 + 2 * t], ST[:, 56 + t:57 + t], 1.0 / 192, ALU.add, ALU.mult, q, T["ssr"])
                q = ts(VE, ST[:, 36:40], ST[:, 36:40], EPS, None, ALU.add, None, q2)
                yield
                q = power(ST[:, 40:44], ST[:, 36:40], 4, q)
                q1 = tt(PO, kn, kn, ST[:, 40:44].rearrange("p (a b) -> p a b", b=1).to_broadcast([128, 4, 128]), ALU.mult, q)
                for t in range(2):
                    q1 = tt(PO, KR2[:, 2 * t:2 * t + 2, :], RK[:, t:t + 1, :].to_broadcast([128, 2, 64]),
                            ST[:, 40 + 2 * t:42 + 2 * t].rearrange("p (a b) -> p a b", b=1).to_broadcast([128, 2, 64]), ALU.mult, q, T["rk"],
                            att.get("rkr"))
                yield
                while "qn" not in att:
                    yield
                qn = att.pop("qn")
                tt_tok = []
                for which in range(4):
                    b, pb, wb = bank()
                    rows = 128 if which < 2 else 64
                    for h in range(2):
                        for t in range(2):
                            o = pb[0:rows, (2 * h + t) * 128:(2 * h + t + 1) * 128]
                            src = (QN[:, t, h * 192:h * 192 + 128], KV[:, t, h * 256:h * 256 + 128], QR[:, 2 * t + h, :], KR2[:, 2 * t + h, :])[which]
                            last = tr(o, src, IDN, wb, qn, q1, inc=(h == 1 and t == 1))
                    if which == 0:
                        te = ts(VE, TT[0:rows, which, :], pb[0:rows, :], GQ[:, 1 + l:2 + l], None, ALU.mult, None, last, att.get("rT"))
                    else:
                        te = copy_act(TT[0:rows, which, :], pb[0:rows, :], last, att.get("rT"))
                    tt_tok.append(te)
                    t_slots.release(b, te)
                att["rq"] = att["rkr"] = last
                att["busyq"] = False
                yield
                isc = 192.0 ** -0.5
                ex = []
                for h in range(2):
                    b, pb, wb = bank()
                    for t, (o, n) in enumerate(((0, 128), (128, 256))):
                        qs, ks = slice(h * 256 + t * 128, h * 256 + t * 128 + 128), slice(h * 256, h * 256 + n)
                        mm(pb[:, o:o + n], TT[:, 0, qs], TT[:, 1, ks], True, False, wb, tt_tok)
                        last = mm(pb[:, o:o + n], TT[0:64, 2, qs], TT[0:64, 3, ks], False, True, inc=(t == 1))
                    dg = SCO[:, h, :].rearrange("p (a b) -> p a b", b=128)[:, 0:3:2, :]
                    pd = pb[:, 0:384].rearrange("p (a b) -> p a b", b=128)[:, 0:3:2, :]
                    ta = tt(VE, dg, pd, NM.rearrange("p (a b) -> p a b", a=1).to_broadcast([128, 2, 128]), ALU.add, last, att.get("rS"))
                    tb = copy_dve(SCO[:, h, 128:256], pb[:, 128:256], last, att.get("rS"))
                    t_slots.release(b, tb)
                    m = ST[:, 44 + 2 * h:46 + 2 * h]
                    red(m[:, 0:1], SCO[:, h, 0:128], ALU.max, ta, tb)
                    tm = red(m[:, 1:2], SCO[:, h, 128:384], ALU.max, ta, tb)
                    tm = ts(VE, m, m, -isc, None, ALU.mult, None, tm)
                    act(SCO[:, h, 0:128], SCO[:, h, 0:128], ACT.Exp, tm, scale=isc, bias=m[:, 0:1], accum_out=ST[:, 48 + 2 * h:49 + 2 * h])
                    te = act(SCO[:, h, 128:384], SCO[:, h, 128:384], ACT.Exp, scale=isc, bias=m[:, 1:2], accum_out=ST[:, 49 + 2 * h:50 + 2 * h])
                    ex.append(te)
                ri = VE.do(lambda e: e.reciprocal(ST[:, 52:56], ST[:, 48:52]), ex)
                att["rT"] = last
                yield
                pt = []
                for h in range(2):
                    b, pb, wb = bank()
                    for i in range(3):
                        last = tr(pb[:, i * 128:(i + 1) * 128], SCO[:, h, i * 128:(i + 1) * 128], IDN, wb, ex[h], inc=(i == 2))
                    te = copy_act(PTB[:, h, :], pb[:, 0:384], last, att.get("rP"))
                    t_slots.release(b, te)
                    pt.append(te)
                att["rS"] = last
                yield
                while ("g", 6 + g // 2) not in T:
                    yield
                b, pb, wb = bank()
                for h in range(2):
                    v0, v1 = (KV[:, t, h * 256 + 128:h * 256 + 256] for t in range(2))
                    o0, o1 = (pb[:, (2 * t + h) * 128:(2 * t + h + 1) * 128] for t in range(2))
                    mm(o0, PTB[:, h, 0:128], v0, True, True, wb, pt)
                    mm(o1, PTB[:, h, 128:256], v0, True, False)
                    last = mm(o1, PTB[:, h, 256:384], v1, False, True, inc=(h == 1))
                att["rkv"] = att["rP"] = last
                fs, wf = f_slots.take()
                f = FB[:, fs, :]
                for t in range(2):
                    for h in range(2):
                        s = slice((2 * t + h) * 128, (2 * t + h + 1) * 128)
                        te = stt(f[:, s], pb[:, s], ST[:, 52 + 2 * h + t:53 + 2 * h + t], SMG[:, t, (2 * g + h) * 128:(2 * g + h + 1) * 128],
                                 ALU.mult, ALU.mult, last, wf, ri, T["g", 6 + g // 2])
                t_slots.release(b, te)
                yield
                flast, tl = flip(lambda kt, t: f[:, (2 * t + kt - 2 * g) * 128:(2 * t + kt - 2 * g + 1) * 128], (2 * g, 2 * g + 1), te, go.tok,
                                 BH[:, 2 * g:2 * g + 2, :].rearrange("p a b -> p (a b)"), BL[:, 2 * g:2 * g + 2, :].rearrange("p a b -> p (a b)"),
                                 plain)
                f_slots.release(fs, flast)
                att["busyk"] = False

            def after_z():
                SC.wait(gz.end)
                SC.ops.append(lambda e: e.dma_start(BR[0:1, :], A["b_pw_2"][l:l + 1, :]).then_inc(s_br, 16))
                while "conv" not in T:
                    yield
                yield from layernorm()
                for j in range(4):
                    b, pb, wb = bank()
                    for i in range(4):
                        gc = MOD[:, l, 32 + 4 * j + i:33 + 4 * j + i].to_broadcast([128, 128])
                        last = mm(pb[:, i * 128:(i + 1) * 128], gc, IDN, True, True, wb, inc=(i == 3))
                    T["G", j] = copy_act(G[:, j * 512:(j + 1) * 512], pb, last)
                    t_slots.release(b, T["G", j])
                    yield

            def p_done(c, p, tok):
                for t in range(2):
                    te = tt(VE, MP[:, t, :], P[:, 2 * p + t, :], SCG[:, t, c * 512:(c + 1) * 512], ALU.mult, tok, T["g", 8 + c], T.get("mp"))
                pairs.release(p, te)
                yield
                for i in (0, 2):
                    k = 8 + 4 * c + i
                    T["mp"], _ = flip(lambda kt, t: MP[:, t, (kt - 8 - 4 * c) * 128:(kt - 7 - 4 * c) * 128], (k, k + 1), te, go.tok,
                                      BH[:, k:k + 2, :].rearrange("p a b -> p (a b)"), BL[:, k:k + 2, :].rearrange("p a b -> p (a b)"), plain)
                    if i == 0:
                        yield

            def o_done(c, p, tok):
                for t in range(2):
                    fs, wf = f_slots.take()
                    te = tt(VE, FB[:, fs, :], P[:, 2 * p + t, :], G[:, c * 512:(c + 1) * 512], ALU.mult, tok, T["G", c], wf)
                    o = X[:, t, c * 512:(c + 1) * 512]
                    xs[(c, t)] = tx = tt(PO, o, o, FB[:, fs, :], ALU.add, te, xs[(c, t)], rms["n"])
                    f_slots.release(fs, tx)
                pairs.release(p, te)
                if l == 0:
                    x_square(c)
                if l == 1:
                    for t in range(2):
                        SP.wait(xs[(c, t)])
                    SP.ops.append(lambda e: e.dma_start(out[0].rearrange("(t p) d -> p t d", p=128)[:, :, c * 512:(c + 1) * 512],
                                                        X[:, :, c * 512:(c + 1) * 512]).then_inc(s_out, 16))
                return
                yield

            def bias(o, c):
                mm(o, ONE[0:1, :], BR[0:1, c * 512:(c + 1) * 512], True, False, (s_br, 16 * (l + 1)))

            gz.done, gq.done, gk.done, gp.done, go.done = z_done, q_done, kv_done, p_done, o_done
            gp.bias = bias
            w_in, w_o = A["w_in_2"][l], A["w_out_2"][l]
            zc = [(1856, 512), (2880, 512), (2368, 512), (3392, 512), (0, 512), (512, 320), (832, 512), (1344, 512), (3904, 512), (4416, 512)]

            def z_units(c):
                c0, w = zc[c]
                for k in range(0, 16, 2):
                    unit(gz, c, w_in, k * 128, k, 2, c0, w, k == 0, k == 14)

            def up_units(g):
                for k in (0, 2):
                    unit(gq, g, A["w_q_up_2"][l], k * 128, k, 2, 384 * g, 384, k == 0, k == 2)
                unit(gk, g, A["w_kv_up_2"][l], 0, 0, 2, 512 * g, 512, True, True)

            for c in range(7):
                z_units(c)
            up_units(0)
            z_units(7)
            up_units(1)
            z_units(8)
            up_units(2)
            z_units(9)
            gz.last_unit = plan[-1]
            gz.fence = lambda: spawn(after_z())
            up_units(3)
            for c in range(2):
                for k in range(0, 8, 2):
                    unit(gp, c, A["w_pw_2"][l], k * 128, k, 2, 512 * c, 512, k == 0, k == 6)

            def o_units(c, ks):
                for k in ks:
                    unit(go, c, w_o, k * 128, k, 2, 512 * c, 512, k == 8, k == 6)

            o_units(0, (8, 10, 12, 14))
            o_units(1, (8, 10, 12, 14))
            o_units(0, (0, 2, 4, 6))
            o_units(1, (0, 2, 4, 6))
            for c in (2, 3):
                o_units(c, (8, 10, 12, 14, 0, 2, 4, 6))
            go.last_unit = plan[-1]
            return start, go

        s_out = sem("s_out")
        scl = {}
        gz_free = {}
        UTk = put("UTk", [128, 128], off=oBL + 6 * K)
        RT = put("RT", [128, 256], off=oBL + 6 * K + 512)

        wq, wo = A["sb_w_qkv"][0], A["sb_w_o"][0]
        for j in range(4):
            for kind in range(3):
                for k in range(0, 16, 2):
                    unit(g_qkv, 3 * j + kind, wq, k * 128, k, 2, kind * 2048 + 512 * j, 512, k == 0, k == 14)
        for cs in ((0, 1), (2, 3)):
            for lo, hi in ((0, 12), (12, 16)):
                for c in cs:
                    for k in range(lo, hi, 2):
                        unit(g_wo, c, wo, k * 128, k, 2, 512 * c, 512, k == 0, k == 14)

        def m1_units(e):
            for c in range(2):
                for k in range(0, 16, 2):
                    unit(g_m1, 2 * e + c, A["mlp_w_in"][0], k * 128, k, 2, (2 * e + c) * 512, 512, k == 0, k == 14)

        def m2_units(e):
            for c in range(4):
                for k in range(0, 8, 2):
                    unit(m2[e], c, A["mlp_w_out"][0], e * 1024 + k * 128, k, 2, 512 * c, 512, k == 0, k == 6)

        m1_units(0)
        for e in range(1, 8):
            m1_units(e)
            m2_units(e - 1)
        m2_units(7)
        first_end = len(plan)
        m2[7].last_unit = plan[-1]
        start0, go0 = layer(0)
        start1, go1 = layer(1)
        gz_free[0] = lambda: g_m1.end
        gz_free[1] = lambda: go0.end
        m2[7].fence = lambda: spawn(start0())
        go0.fence = lambda: spawn(start1())

        adas = [(l, pc, kt) for l in range(2) for pc in range(6) for kt in range(16)]
        for i, u in enumerate(plan):
            items.append(("w", u))
            if 12 <= i < first_end and i % 2 == 1 and adas:
                items.append(("a", adas.pop(0)))
            if i == first_end - 8:
                items += [("a", a) for a in adas]
                adas = []
        for _ in range(NR):
            issue_dma()
        spawn(x_start())
        spawn(load_vectors())
        run()
        SP.ops.append(lambda e: e.wait_ge(s_out, 64))

        block = ctx.enter_context(nc.Block())

        @block.sync
        def _(e):
            for f in SP.ops:
                f(e)

        @block.scalar
        def _(e):
            for f in SC.ops:
                f(e)

        @block.vector
        def _(e):
            for f in VE.ops:
                f(e)

        @block.gpsimd
        def _(e):
            for f in PO.ops:
                f(e)

        @block.tensor
        def _(e):
            for f in PE.ops:
                f(e)


def constants():
    c = np.zeros((128, 6 * 128 + 33), np.float32)
    p, f = np.arange(128)[:, None], np.arange(128)[None, :]
    c[:, 0:128] = p == f
    c[:, 128:256] = p < f
    c[:, 256:384] = -(p > f).astype(np.float32)
    c[:, 384:512] = -1.0
    c[:, 512:640] = np.where(f <= p, 0.0, -1e30)
    c[:, 640:768] = 1.0
    e = np.arange(0, 64, 2, dtype=np.float32) / np.float32(64)
    c[:, 768:800] = np.float32(1.0) / np.power(np.float32(10000.0), e)
    c[:, 800] = -0.5
    return c


_INS = ["x", "norm_mix_g", "norm_mlp_g", "sb_w_qkv", "sb_q_norm_g", "sb_k_norm_g", "sb_w_o", "mlp_w_in", "mlp_w_out",
        "c_2", "positions_2", "ada_w_2", "ada_b_2", "norm_g_2", "w_in_2", "q_lat_g_2", "w_q_up_2", "kv_lat_g_2",
        "w_kv_up_2", "q_norm_g_2", "k_norm_g_2", "glu_b_2", "dw_w_2", "dw_b_2", "conv_ln_g_2", "conv_ln_b_2",
        "w_pw_2", "b_pw_2", "w_out_2"]


def kernel(**inputs):
    import concourse.bacc as _bacc
    from concourse.bass_utils import run_bass_kernel_spmd as _run

    nc = _bacc.Bacc("TRN2", target_bir_lowering=False, num_devices=1)
    arrays, args = {}, {}
    given = {name: np.ascontiguousarray(inputs[name]) for name in _INS}
    given["consts"] = constants()
    for name, a in given.items():
        arrays[f"in_{name}_dram"] = a
        args[name] = nc.dram_tensor(f"in_{name}_dram", a.shape, mybir.dt.from_np(a.dtype), kind="ExternalInput").ap()
    out = nc.dram_tensor("out_0_dram", (1, 256, 2048), F32, kind="ExternalOutput").ap()
    build(nc, args, out)
    r = _run(nc, [arrays], core_ids=[0])
    return r.results[0]["out_0_dram"]
```

```python
import numpy as np
import concourse.bass as bass
from concourse import mybir
from contextlib import ExitStack

F32 = mybir.dt.float32
F32R = mybir.dt.float32r
I32 = mybir.dt.int32
ALU = mybir.AluOpType
ACT = mybir.ActivationFunctionType
AXX = mybir.AxisListType.X
K = 1024
EPS = 1e-6
D = 2048
CONVP = 0


class Engine:

    def __init__(self, sem):
        self.sem, self.n, self.seen, self.ops = sem, 0, {}, []

    def wait(self, *tokens):
        for t in tokens:
            if isinstance(t, list):
                self.wait(*t)
            elif t is not None and self.seen.get(t[0], 0) < t[1]:
                self.seen[t[0]] = t[1]
                self.ops.append(lambda e, s=t[0], v=t[1]: e.wait_ge(s, v))

    def do(self, fn, *after, inc=True):
        self.wait(*after)
        if inc:
            self.n += 1
            self.ops.append(lambda e: fn(e).then_inc(self.sem, 1))
            return (self.sem, self.n)
        self.ops.append(fn)
        return None

    def last(self):
        return (self.sem, self.n) if self.n else None


class Slots:

    def __init__(self, n):
        self.n, self.i, self.rel = n, 0, [[] for _ in range(n)]

    def take(self):
        s = self.i % self.n
        self.i += 1
        assert self.rel[s] is not None, "slot still held"
        w, self.rel[s] = self.rel[s], None
        return s, w

    def release(self, s, *tokens):
        self.rel[s] = list(tokens)


def build(nc, A, out):
    ctx = ExitStack()
    with ctx:
        sem = lambda n: ctx.enter_context(nc.semaphore(n))
        PE, SC, VE, PO, SP = (Engine(sem("s_" + n)) for n in ("pe", "act", "dve", "pool", "sp"))
        base = 16512
        at = [base]

        def put(name, shape, dt=F32, off=None):
            size = int(np.prod(shape[1:])) * 4
            if off is None:
                off = at[0]
                at[0] += (size + 31) // 32 * 32
            return nc.alloc_sbuf_tensor_at(name, shape, dt, offset=off)

        NR, NH, LA = 5, 4, 3
        RAW = put("RAW", [128, NR, 1024])
        WH = put("WH", [128, NH, 1024], F32R)
        WL = put("WL", [128, NH, 1024], F32R)
        X = put("X", [128, 2, D])
        oA = at[0]
        AH = put("AH", [128, 16, 256], F32R)
        AL = put("AL", [128, 16, 256], F32R)
        oBH = at[0]
        BH = put("BH", [128, 16, 256], F32R)
        oBL = at[0]
        BL = put("BL", [128, 16, 256], F32R)
        FB = put("FB", [128, 4, 512])
        PB = put("PB", [128, 4, 256])
        CST = put("CST", [128, 6 * 128 + 32 + 1])
        VC = put("VC", [128, 276])
        DW = put("DW", [128, 2, 8, 31])
        MOD = put("MOD", [128, 2, 48])
        TRG = put("TRG", [128, 4, 64])
        CS = put("CS", [128, 2, 2, 32])
        TQ = put("TQ", [128, 4, 2, 32])
        TK = put("TK", [128, 4, 2, 32])
        CC = put("CC", [128, 16])
        ST = put("ST", [128, 96])
        SCL = put("SCL", [128, 16])
        GQ = put("GQ", [128, 4])
        oS = at[0]
        assert oS + 9152 + 44 * K <= 229344, (229344 - oS) / K

        IDN = CST[:, 0:128]
        MS = CST[:, 128:256]
        UN = CST[:, 256:384]
        NG = CST[:, 384:512]
        NM = CST[:, 512:640]
        ONE = CST[:, 640:768]
        INVF = CST[:, 768:800]
        MH = CST[:, 800:801]

        N = put("N", [128, 2, D], off=oS)
        QK = put("QK", [128, 2, 2, 512], off=oS)
        SQ = put("SQ", [128, 1024], off=oS + 8 * K)
        V1 = put("V1", [128, 2, 512], off=oS + 12 * K)
        QT1 = put("QT1", [128, 2, 4, 256], off=oS + 16 * K)
        TL = put("TL", [128, 4, 384], off=oS + 24 * K)
        TA = put("TA", [128, 4, 384], off=oS + 30 * K)
        TN = put("TN", [128, 4, 384], off=oS + 36 * K)
        ACC2 = put("ADA", [128, 2, 1024], off=oS + 44 * K)
        RN = put("RN", [128, 2, 2, 512], off=oS + 16 * K)
        VR = put("VR", [128, 3, 128], off=oS + 24 * K)
        DR = put("DR", [31, 2, 1024], off=oS + 26 * K)
        PI = put("PI", [128, 2], I32, off=oS + 34 * K)
        AG = put("AG", [128, 8, 64], off=oS + 35 * K)
        UT = put("UT", [128, 8, 286], off=oS)
        LNS = put("LNS", [128, 4, 256], off=oS)
        o2 = oS + 9152
        SMG = put("SMG", [128, 2, 1024], off=o2)
        SCG = put("SCG", [128, 2, 1024], off=o2 + 8 * K)
        KLH = put("KLH", [128, 2, 256], F32R, off=o2 + 16 * K)
        KLL = put("KLL", [128, 2, 256], F32R, off=o2 + 18 * K)
        KV = put("KV", [128, 2, 512], off=o2 + 20 * K)
        QN = put("QN", [128, 2, 384], off=o2 + 24 * K)
        QR = put("QR", [128, 4, 64], off=o2 + 27 * K)
        KR2 = put("KR2", [128, 4, 64], off=o2 + 28 * K)
        TT = put("TTr", [128, 4, 512], off=o2 + 29 * K)
        SCO = put("SCO", [128, 2, 384], off=o2 + 37 * K)
        PTB = put("PTB", [128, 2, 384], off=o2 + 40 * K)
        KR = put("KR", [128, 2, 64], off=o2 + 43 * K)
        RK = put("RK", [128, 2, 64], off=o2 + 43 * K + 512)
        ULH = put("ULH", [128, 8, 256], F32R, off=oA)
        ULL = put("ULL", [128, 8, 256], F32R, off=oA + 8 * K)
        G = put("G", [128, D], off=oA + 16 * K)
        MP = put("MP", [128, 2, 512], off=oA + 24 * K)
        BR = put("BR", [1, 1024], off=oA + 28 * K)
        UV = put("UV", [128, 2, 512], off=oBH)
        UG = put("UG", [128, 2, 512], off=oBH + 4 * K)
        CA = put("CA", [128, 8, 256], off=oBH + 8 * K)
        NQ = put("NQ", [128, 2, 512], off=oBL)
        NK = put("NK", [128, 2, 256], off=oBL + 4 * K)
        QLH = put("QLH", [128, 4, 256], F32R, off=oBL + 8 * K)
        QLL = put("QLL", [128, 4, 256], F32R, off=oBL + 12 * K)

        P = ctx.enter_context(nc.psum_tensor("P", [128, 8, 512], F32))

        f_slots = Slots(4)
        t_slots = Slots(4)
        p_slots = Slots(4)
        pairs = Slots(2)

        def bank():
            s, w = t_slots.take()
            return s, P[:, 4 + s, :], w

        def copy_act(o, i, *w):
            return SC.do(lambda e: e.activation(o, i, ACT.Copy), *w)

        def copy_dve(o, i, *w):
            return VE.do(lambda e: e.tensor_copy(o, i), *w)

        def act(o, i, f, *w, **k):
            return SC.do(lambda e: e.activation(o, i, f, **k), *w)

        def tt(E, o, a, b, op, *w):
            return E.do(lambda e: e.tensor_tensor(o, a, b, op), *w)

        def ts(E, o, a, s1, s2, op0, op1, *w):
            if s2 is None:
                return E.do(lambda e: e.tensor_scalar(o, a, s1, None, op0), *w)
            return E.do(lambda e: e.tensor_scalar(o, a, s1, s2, op0, op1), *w)

        def stt(o, a, s, b, op0, op1, *w):
            return VE.do(lambda e: e.scalar_tensor_tensor(out=o, in0=a, scalar=s, in1=b, op0=op0, op1=op1), *w)

        def red(o, a, op, *w):
            return VE.do(lambda e: e.tensor_reduce(o, a, AXX, op), *w)

        def mm(o, l, r, st, sp, *w, inc=False, **k):
            return PE.do(lambda e: e.matmul(o, l, r, start=st, stop=sp, **k), *w, inc=inc)

        def tr(o, i, ident, *w, inc=False):
            return PE.do(lambda e: e.transpose(o, i, ident), *w, inc=inc)

        def power(o, ms, n, *w):
            return tt(PO, o, ms, MH.to_broadcast([128, n]), ALU.pow, *w)

        def split(f, fs, tok, H, L, *w):
            th = copy_act(H, f, tok, *w)
            tl = tt(VE, L, f, H.bitcast(F32), ALU.subtract, th, tok, *w)
            f_slots.release(fs, tl)
            return tl

        def two(T, k):
            return T[:, k:k + 2, :].rearrange("p a b -> p (a b)")

        def flip(src, kts, wsrc, done, H, L, evac, *w, later=None):
            b, pb, wb = bank()
            for i, kt in enumerate(kts):
                for t in range(2):
                    last = tr(pb[:, (2 * i + t) * 128:(2 * i + t + 1) * 128], src(kt, t), IDN, wb, wsrc, c_tok,
                              inc=(i == 1 and t == 1))
            fs, wf = f_slots.take()
            f = FB[:, fs, :]
            te = evac(f, pb, kts, [last, wf])
            t_slots.release(b, te)
            th = copy_act(H, f, te, *w)

            def low():
                tl = tt(VE, L, f, H.bitcast(F32), ALU.subtract, th, te, *w)
                f_slots.release(fs, tl)
                for kt in kts:
                    done[kt] = tl

            if later is None:
                low()
            else:
                later.append(low)
            return last, th

        def flips(src, ks, wsrc, done, H, L, evac, *w, first=False, late=False):
            later = []
            for n, k in enumerate(ks):
                if later and not late:
                    later.pop(0)()
                out_ = flip(src, (k, k + 1), wsrc(k), done, two(H, k), two(L, k), evac(n), *w, later=None if first and n == 0 else later)
                if late and n:
                    later.pop(0)()
                yield out_
            later.pop(0)()

        def affine(s, b, E):
            def go(f, pb, kts, w):
                for i, kt in enumerate(kts):
                    o, q = f[:, i * 256:(i + 1) * 256], pb[:, i * 256:(i + 1) * 256]
                    if E is SC and b is None:
                        te = act(o, q, ACT.Copy, w, scale=s[:, kt:kt + 1])
                    elif E is SC:
                        te = act(o, q, ACT.Identity, w, scale=s[:, kt:kt + 1], bias=b[:, kt:kt + 1])
                    elif b is None:
                        te = ts(VE, o, q, s[:, kt:kt + 1], None, ALU.mult, None, w)
                    else:
                        te = ts(VE, o, q, s[:, kt:kt + 1], b[:, kt:kt + 1], ALU.mult, ALU.add, w)
                return te
            return go

        def plain(f, pb, kts, w):
            return copy_act(f, pb, w)

        def squared(f, pb, kts, w):
            return act(f, pb, ACT.Square, w)

        s_c, s_v, s_g, s_br = sem("s_c"), sem("s_v"), sem("s_g"), sem("s_br")
        s_x = [sem(f"s_x{c}") for c in range(4)]
        c_tok = (s_c, 16)
        x_in = A["x"][0].rearrange("(t p) d -> p t d", p=128)

        def load_x(c):
            SP.ops.append(lambda e: e.dma_start(X[:, :, c * 512:(c + 1) * 512], x_in[:, :, c * 512:(c + 1) * 512]).then_inc(s_x[c], 16))

        SC.ops.append(lambda e: e.dma_start(VR[0:16, 0, :], A["norm_mix_g"].rearrange("a (r p) -> (a r) p", p=128)).then_inc(s_g, 16))
        SC.ops.append(lambda e: e.dma_start(CST[:, :], A["consts"]).then_inc(s_c, 16))
        SC.ops.append(lambda e: e.preload_act_table_set("silu_and_others"))
        rows = [[("norm_mlp_g", 16), ("norm_g_2", 32), ("q_lat_g_2", 8), ("kv_lat_g_2", 4),
                 ("conv_ln_g_2", 16), ("conv_ln_b_2", 16), ("sb_q_norm_g", 1), ("sb_k_norm_g", 1),
                 ("q_norm_g_2", 2), ("k_norm_g_2", 2)],
                [("dw_b_2", 16), ("glu_b_2", 32), ("c_2", 16)], [("ada_b_2", 96)]]
        col, nrow, vload, at_col = {"norm_mix_g": VC[:, 0:16]}, [16, 0, 0], [], [0, 114, 178]
        for g, names in enumerate(rows):
            for name, n in names:
                r = nrow[g]
                src = A[name][:, 0:128] if name in ("q_norm_g_2", "k_norm_g_2") else A[name].rearrange("a (r p) -> (a r) p", p=128)
                vload.append((VR[r:r + n, g, :], src, {}))
                col[name] = VC[:, at_col[g] + r:at_col[g] + r + n]
                nrow[g] = r + n
        assert nrow == [114, 64, 96]
        vload.append((DR[:, :, :], A["dw_w_2"].rearrange("l k c -> k l c"), {}))
        vload.append((PI[:, :], A["positions_2"].rearrange("a (t p) -> p (a t)", p=128), {"allow_slow_non_contiguous": True}))
        for l in range(2):
            vload.append((TRG[:, 2 * l, :], A["q_norm_g_2"][l:l + 1, 128:192].to_broadcast([128, 64]), {}))
            vload.append((TRG[:, 2 * l + 1, :], A["k_norm_g_2"][l:l + 1, 128:192].to_broadcast([128, 64]), {}))
        v_tok = (s_v, 16 * len(vload))

        b, pb, wb = bank()
        last = tr(pb[:, 0:16], VR[0:16, 0, :], CST[0:16, 0:16], (s_g, 16), c_tok, inc=True)
        mg_tok = copy_dve(VC[:, 0:16], pb[:, 0:16], last)
        t_slots.release(b, mg_tok)
        C = {}

        def load_vectors():
            for _ in range(8):
                yield
            b, pb, wb = bank()
            for g in range(3):
                n = nrow[g]
                last = tr(pb[:, g * 128:g * 128 + n], VR[0:n, g, :], CST[0:n, 0:n], v_tok, c_tok, wb, inc=(g == 2))
            copy_dve(VC[:, 16:114], pb[:, 16:114], last)
            copy_dve(VC[:, 114:178], pb[:, 128:192], last)
            C["vc"] = vc_tok = copy_dve(VC[:, 178:274], pb[:, 256:352], last)
            t_slots.release(b, vc_tok)
            C["cc"] = act(CC[:, :], col["c_2"], ACT.Silu, vc_tok)
            ts(VE, GQ[:, 0:1], col["sb_q_norm_g"], 128.0 ** -0.5, None, ALU.mult, None, vc_tok)
            C["gq"] = tt(VE, GQ[:, 1:3], col["q_norm_g_2"], col["k_norm_g_2"], ALU.mult, vc_tok)
            b, pb, wb = bank()
            for l in range(2):
                for c in range(8):
                    o = (l * 8 + c) * 31
                    last = tr(pb[:, o:o + 31], DR[0:31, l, c * 128:(c + 1) * 128], CST[0:31, 0:31], wb, v_tok, inc=(l == 1 and c == 7))
            C["dw"] = copy_dve(DW[:, :, :, :].rearrange("p a b c -> p (a b c)"), pb[:, 0:496], last)
            t_slots.release(b, C["dw"])
            yield
            yield
            posf, ang, kk = AG[:, 0, 0:2], AG[:, 1, :], AG[:, 2, :]
            t0 = copy_dve(posf, PI[:, :], v_tok)
            for t in range(2):
                t1 = ts(VE, ang[:, 32 * t:32 * t + 32], INVF, posf[:, t:t + 1], None, ALU.mult, None, t0, c_tok)
            t1 = ts(VE, kk, ang, float(np.float32(1 / (2 * np.pi))), None, ALU.mult, None, t1)
            t1 = ts(VE, kk, kk, 12582912.0, None, ALU.add, None, t1)
            t1 = ts(VE, kk, kk, -12582912.0, None, ALU.add, None, t1)
            r1, cur = 2 * np.pi, ang
            for i in range(3):
                part = np.float32(r1)
                if i < 2:
                    part = np.uint32(part.view(np.uint32) & np.uint32(0xFFFF8000)).view(np.float32)
                r1 -= float(part)
                t1 = stt(AG[:, 3 + i, :], kk, -float(part), cur, ALU.mult, ALU.add, t1)
                cur = AG[:, 3 + i, :]
            t1 = ts(VE, cur, cur, float(np.float32(3.1415925)), float(np.float32(-3.1415925)), ALU.min, ALU.max, t1)
            sv = CS[:, 1, :, :].rearrange("p t f -> p (t f)")
            cv = CS[:, 0, :, :].rearrange("p t f -> p (t f)")
            yield
            act(sv, cur, ACT.Sin, t1)
            t2 = ts(VE, AG[:, 6, :], cur, -1.0, None, ALU.mult, None, t1)
            t2 = tt(VE, AG[:, 7, :], cur, AG[:, 6, :], ALU.max, t2)
            t2 = ts(VE, AG[:, 6, :], AG[:, 7, :], -1.0, float(np.float32(np.pi / 2)), ALU.mult, ALU.add, t2)
            yield
            C["cs"] = act(cv, AG[:, 6, :], ACT.Sin, t2)
            SC.ops.append(lambda e: e.preload_act_table_set("natural_log_exp_and_others"))

        class Gemm:
            def __init__(self, H, L, done):
                self.H, self.L, self.done, self.tok, self.bias, self.fence = H, L, done, {}, None, None
                self.end, self.last_unit, self.pair = None, None, {}

        plan = []

        def unit(g, c, src, r0, k0, nk, c0, w, st, sp):
            plan.append(dict(g=g, c=c, src=src, r0=r0, k0=k0, nk=nk, c0=c0, w=w, st=st, sp=sp))

        jobs = []

        def spawn(gen):
            jobs.append(gen)

        def pump():
            for j in list(jobs):
                try:
                    next(j)
                except StopIteration:
                    jobs.remove(j)

        raw_sem = [sem(f"s_raw{i}") for i in range(NR)]
        items, raw_free, state = [], {}, dict(dma=0, item=0)
        hl_slots = Slots(NH)
        wtok = {}

        def issue_dma():
            i = state["dma"]
            if i >= len(items):
                return
            state["dma"] += 1
            kind, u = items[i]
            s = i % NR
            SP.wait(raw_free.get(i - NR))
            if kind == "w":
                dst = RAW[:, s, 0:u["nk"] * u["w"]].rearrange("p (k n) -> p k n", k=u["nk"])
                src = u["src"][u["r0"]:u["r0"] + 128 * u["nk"], u["c0"]:u["c0"] + u["w"]].rearrange("(k p) n -> p k n", p=128)
            else:
                l, pc, kt = u
                dst = RAW[:, s, :]
                src = A["ada_w_2"][l, kt * 128:(kt + 1) * 128, pc * 1024:(pc + 1) * 1024]
            SP.ops.append(lambda e: e.dma_start(dst, src).then_inc(raw_sem[s], 16))

        ada_slots = Slots(2)
        ada = dict(tok=None, slot=0, w=None)
        mod_tok = {}

        def ada_reduce(l, pc, slot, tok):
            yield
            yield
            b, pb, wb = bank()
            for j in range(8):
                last = mm(pb[:, j:j + 1], ACC2[:, slot, j * 128:(j + 1) * 128], ONE[:, 0:1], True, True, wb, tok, c_tok, inc=(j == 7))
            ada_slots.release(slot, last)
            o = 8 * pc
            te = tt(VE, MOD[:, l, o:o + 8], pb[:, 0:8], col["ada_b_2"][:, 48 * l + o:48 * l + o + 8], ALU.add, last, C["vc"])
            t_slots.release(b, te)
            mod_tok[l] = te
            yield

        def take_item():
            i = state["item"]
            state["item"] += 1
            kind, u = items[i]
            s = i % NR
            there = (raw_sem[s], 16 * (i // NR + 1))
            if kind == "a":
                l, pc, kt = u
                if kt == 0:
                    ada["slot"], ada["w"] = ada_slots.take()
                acc = ACC2[:, ada["slot"], :]
                sc = CC[:, kt:kt + 1]
                if kt == 0:
                    t = ts(VE, acc, RAW[:, s, :], sc, None, ALU.mult, None, there, ada["w"], C["cc"])
                else:
                    t = stt(acc, RAW[:, s, :], sc, acc, ALU.mult, ALU.add, there, ada["tok"])
                ada["tok"] = t
                raw_free[i] = t
                if kt == 15:
                    spawn(ada_reduce(l, pc, ada["slot"], t))
            else:
                n = u["nk"] * u["w"]
                h, wh = hl_slots.take()
                r, H, L = RAW[:, s, 0:n], WH[:, h, 0:n], WL[:, h, 0:n]
                th = copy_act(H, r, there, wh)
                tl = tt(VE, L, r, H.bitcast(F32), ALU.subtract, there, th)
                raw_free[i] = tl
                wtok[id(u)] = (h, tl, th)
            issue_dma()
            return kind

        def run():
            w_at = [0]

            def prefetch(to):
                while w_at[0] < min(to, len(plan)):
                    if take_item() == "w":
                        w_at[0] += 1

            for i, u in enumerate(plan):
                if i == 0:
                    prefetch(1)
                    pump()
                prefetch(min(i + 1 + LA, 2 * i + 2))
                g = u["g"]
                for k in range(u["nk"]):
                    while u["k0"] + k not in g.tok:
                        assert jobs
                        pump()
                if u["st"]:
                    while pairs.rel[pairs.i % 2] is None:
                        if pairs.rel[(pairs.i + 1) % 2] is not None:
                            pairs.i += 1
                        else:
                            pump()
                    p, wp = pairs.take()
                    g.pair[u["c"]] = p
                    PE.wait(wp)
                p = g.pair[u["c"]]
                st = u["st"]
                if st and g.bias:
                    for t in range(2):
                        g.bias(P[:, 2 * p + t, 0:u["w"]], u["c"])
                    st = False
                h, tl, th = wtok[id(u)]
                W = u["w"]
                PE.wait(th, tl)
                for k in range(u["nk"]):
                    kt = u["k0"] + k
                    PE.wait(g.tok[kt])
                    wh, wl = WH[:, h, k * W:(k + 1) * W], WL[:, h, k * W:(k + 1) * W]
                    for t in range(2):
                        o = P[:, 2 * p + t, 0:W]
                        xh, xl = g.H[:, kt, t * 128:(t + 1) * 128], g.L[:, kt, t * 128:(t + 1) * 128]
                        end = k == u["nk"] - 1
                        mm(o, xh, wh, st and k == 0, False)
                        mm(o, xh, wl, False, False)
                        last = mm(o, xl, wh, False, u["sp"] and end, inc=(end and t == 1))
                hl_slots.release(h, last)
                g.end = last
                if u["sp"]:
                    spawn(g.done(u["c"], p, last))
                pump()
                if g.fence and i + 1 < len(plan) and u is g.last_unit:
                    g.fence()
            while jobs:
                pump()

        xs = {(c, t): (s_x[c], 16) for c in range(4) for t in range(2)}
        rms = {}

        def x_square(c):
            for t in range(2):
                fs, wf = f_slots.take()
                q = act(FB[:, fs, :], X[:, t, c * 512:(c + 1) * 512], ACT.Square, xs[(c, t)], wf, rms.get("used"),
                        accum_out=ST[:, 64 + 4 * t + c:65 + 4 * t + c])
                f_slots.release(fs, q)
            rms[c] = q
            if all(i in rms for i in range(4)):
                q = red(ST[:, 72:74], ST[:, 64:72].rearrange("p (a b) -> p a b", b=4), ALU.add, [rms.pop(i) for i in range(4)])
                q = ts(VE, ST[:, 72:74], ST[:, 72:74], 1.0 / D, EPS, ALU.mult, ALU.add, q)
                rms["tok"] = power(ST[:, 74:76], ST[:, 72:74], 2, q, c_tok, rms.get("read"))

        def x_flip(dst, gain, c, *w):
            for last, _ in flips(lambda kt, tk: X[:, tk, kt * 128:(kt + 1) * 128], (4 * c, 4 * c + 2), lambda k: [xs[(c, 0)], xs[(c, 1)]],
                                 dst.tok, dst.H, dst.L, lambda n: affine(gain, None, VE), *w):
                rms["fliptok"] = last
                yield

        def x_start():
            VE.wait(mg_tok)
            for last, _ in flips(lambda kt, tk: X[:, tk, kt * 128:(kt + 1) * 128], range(0, 16, 2), lambda k: [xs[(k // 4, 0)], xs[(k // 4, 1)]],
                                 g_qkv.tok, g_qkv.H, g_qkv.L, lambda n: affine(col["norm_mix_g"], None, (VE, SC)[n % 2]), first=True):
                rms["fliptok"] = last
                yield
            for c in range(4):
                yield
                x_square(c)

        def xprep(dst, scale, bias, *w):
            t = rms["tok"]
            nt = {}

            def normed(j):
                nt[j] = []
                for tk in range(2):
                    n_, x_, r_ = N[:, tk, j * 512:(j + 1) * 512], X[:, tk, j * 512:(j + 1) * 512], ST[:, 74 + tk:75 + tk]
                    if tk:
                        nt[j].append(act(n_, x_, ACT.Copy, t, xs[(j, tk)], *w, scale=r_))
                    else:
                        nt[j].append(ts(VE, n_, x_, r_, None, ALU.mult, None, t, xs[(j, tk)], *w))
            VE.wait(C["scl"])
            normed(0)
            normed(1)
            for n, (last, _) in enumerate(flips(lambda kt, tk: N[:, tk, kt * 128:(kt + 1) * 128], range(0, 16, 2), lambda k: nt[k // 4],
                                                dst.tok, dst.H, dst.L, lambda n: affine(scale, bias, (VE, SC)[n % 2]), *w, late=True)):
                rms["n"] = last
                if n % 2 == 0 and n < 4:
                    normed(n // 2 + 2)
            rms["used"] = rms["read"] = nt[3]
            yield

        qkt = dict(nat=[None, None], T=[None, None], rT=[None, None], V=None, rV=None)
        wo_tok = {}

        def qkv_done(c, p, tok):
            j, kind = c // 3, c % 3
            while "tok" not in rms:
                yield
            if kind == 2:
                for t in range(2):
                    te = act(V1[:, t, :], P[:, 2 * p + t, :], ACT.Copy, tok, qkt["rV"], rms["tok"], scale=ST[:, 74 + t:75 + t])
                pairs.release(p, te)
                qkt["V"] = te
                spawn(sb_heads(j, 0))
                spawn(sb_heads(j, 1))
                return
            nat = QK[:, kind, :, :].rearrange("p t n -> p (t n)")
            for t in range(2):
                te = act(QK[:, kind, t, :], P[:, 2 * p + t, :], ACT.Copy, tok, qkt["nat"][kind], rms["tok"], scale=ST[:, 74 + t:75 + t])
            rms["read"] = te
            pairs.release(p, te)
            n8 = nat.rearrange("p (a d) -> p a d", d=128)
            q = tt(PO, SQ[:, :], nat, nat, ALU.mult, te)
            o = 8 + 24 * kind
            q = red(ST[:, o:o + 8], SQ[:, :].rearrange("p (a d) -> p a d", d=128), ALU.add, q)
            yield
            q = ts(VE, ST[:, o + 8:o + 16], ST[:, o:o + 8], 1.0 / 128, EPS, ALU.mult, ALU.add, q)
            q = power(ST[:, o + 16:o + 24], ST[:, o + 8:o + 16], 8, q)
            q = tt(PO, n8, n8, ST[:, o + 16:o + 24].rearrange("p (a b) -> p a b", b=1).to_broadcast([128, 8, 128]), ALU.mult, q)
            yield
            yield
            yield
            sc = GQ[:, 0:1] if kind == 0 else col["sb_k_norm_g"]
            for hp in range(2):
                b, pb, wb = bank()
                for h in range(2):
                    for t in range(2):
                        last = tr(pb[:, (2 * h + t) * 128:(2 * h + t + 1) * 128], QK[:, kind, t, (2 * hp + h) * 128:(2 * hp + h + 1) * 128],
                                  IDN, wb, q, inc=(h == 1 and t == 1))
                te = act(QT1[:, kind, 2 * hp:2 * hp + 2, :].rearrange("p a b -> p (a b)"), pb, ACT.Copy, last, C["gq"], C["vc"],
                         qkt["rT"][kind], scale=sc)
                t_slots.release(b, te)
            qkt["nat"][kind] = last
            qkt["T"][kind] = te

        tl_rel = [None, None]

        def sb_heads(j, hp):
            while None in qkt["T"]:
                yield
            sl, t1s, nls = [], [], []
            for i in range(2):
                h, s = 2 * hp + i, 2 * hp + i
                b, pb, wb = bank()
                mm(pb[:, 0:256], QT1[:, 1, h, 0:128], QT1[:, 0, h, :], True, True, wb, qkt["T"])
                last = mm(pb[:, 256:384], QT1[:, 1, h, 128:256], QT1[:, 0, h, 128:256], True, True, inc=True)
                z = pb[:, 0:384]
                t = act(TL[:, s, :], z, ACT.Abs, last, tl_rel[hp])
                t = act(TL[:, s, :], TL[:, s, :], ACT.Exp, t, scale=-1.0)
                t = act(TL[:, s, :], TL[:, s, :], ACT.Ln, t, bias=1.0)
                t1 = stt(TA[:, s, :], z, 0.0, TL[:, s, :], ALU.min, ALU.subtract, t, tl_rel[hp])
                t2 = stt(TN[:, s, :], z, 0.0, TL[:, s, :], ALU.max, ALU.add, t, tl_rel[hp])
                t_slots.release(b, t2)
                nd = TN[:, s, :].rearrange("p (a b) -> p a b", b=128)[:, 0:3:2, :]
                t3 = tt(PO, nd, nd, MS.rearrange("p (a b) -> p a b", a=1).to_broadcast([128, 2, 128]), ALU.mult, t2)
                t1s.append(t1)
                nls.append(t3)
            qkt["rT"] = [last, last]
            yield
            yield
            as_ = []
            for i in range(2):
                s = 2 * hp + i
                b, pb, wb = bank()
                mm(pb[:, 0:128], UN, TN[:, s, 0:128], True, True, wb, nls[i])
                mm(pb[:, 128:256], UN, TN[:, s, 128:256], True, False)
                mm(pb[:, 128:256], NG, TN[:, s, 256:384], False, True)
                last = mm(pb[:, 256:384], UN, TN[:, s, 256:384], True, True, inc=True)
                t = tt(VE, TA[:, s, :], pb[:, 0:384], TA[:, s, :], ALU.add, last, t1s[i])
                t_slots.release(b, t)
                t = act(TA[:, s, :], TA[:, s, :], ACT.Exp, t)
                ad = TA[:, s, :].rearrange("p (a b) -> p a b", b=128)[:, 0:3:2, :]
                as_.append(tt(PO, ad, ad, MS.rearrange("p (a b) -> p a b", a=1).to_broadcast([128, 2, 128]), ALU.mult, t))
            yield
            b, pb, wb = bank()
            for i in range(2):
                h, s = 2 * hp + i, 2 * hp + i
                o = pb[:, i * 256:(i + 1) * 256]
                v0, v1 = V1[:, 0, h * 128:(h + 1) * 128], V1[:, 1, h * 128:(h + 1) * 128]
                mm(o[:, 0:128], v0, TA[:, s, 0:128], True, True, wb, as_[i], qkt["V"])
                mm(o[:, 128:256], v0, TA[:, s, 128:256], True, False)
                last = mm(o[:, 128:256], v1, TA[:, s, 256:384], False, True, inc=(i == 1))
            tl_rel[hp] = last
            qkt["rV"] = last
            fs, wf = f_slots.take()
            te = copy_act(FB[:, fs, :], pb, last, wf)
            t_slots.release(b, te)
            kt = 4 * j + 2 * hp
            tl = split(FB[:, fs, :], fs, te, BH[:, kt:kt + 2, :].rearrange("p a b -> p (a b)"), BL[:, kt:kt + 2, :].rearrange("p a b -> p (a b)"))
            g_wo.tok[kt] = g_wo.tok[kt + 1] = tl

        def add_x(c, p, tok):
            for t in range(2):
                o = X[:, t, c * 512:(c + 1) * 512]
                te = tt(VE, o, o, P[:, 2 * p + t, :], ALU.add, tok, xs[(c, t)], rms.get("fliptok"))
                xs[(c, t)] = te
            pairs.release(p, te)
            return
            yield

        def wo_done(c, p, tok):
            yield from add_x(c, p, tok)
            x_square(c)
            yield
            yield
            VE.wait(C["vc"])
            yield from x_flip(g_m1, col["norm_mlp_g"], c, g_qkv.end)

        def last_m2_done(c, p, tok):
            yield from add_x(c, p, tok)
            x_square(c)

        g_qkv = Gemm(AH, AL, qkv_done)
        g_wo = Gemm(BH, BL, wo_done)

        g_m1 = Gemm(AH, AL, None)
        rn_slots = Slots(2)
        m2 = [Gemm(BH[:, 8 * (e % 2):8 * (e % 2) + 8, :], BL[:, 8 * (e % 2):8 * (e % 2) + 8, :], add_x if e < 7 else last_m2_done) for e in range(8)]

        def m1_done(c, p, tok):
            e, cc = c // 2, c % 2
            s, ws = rn_slots.take()
            for t in range(2):
                te = act(RN[:, s, t, :], P[:, 2 * p + t, :], ACT.Relu, tok, ws, rms["tok"], scale=ST[:, 74 + t:75 + t])
            rms["read"] = te
            pairs.release(p, te)
            free = m2[e - 2].end if e >= 2 else g_wo.end
            yield
            for last, _ in flips(lambda kt, t: RN[:, s, t, (kt - 4 * cc) * 128:(kt - 4 * cc + 1) * 128], (4 * cc, 4 * cc + 2), lambda k: te,
                                 m2[e].tok, m2[e].H, m2[e].L, lambda n: squared, free):
                yield
            rn_slots.release(s, last)

        g_m1.done = m1_done

        def layer(l):
            gz = Gemm(AH, AL, None)
            gq = Gemm(QLH, QLL, None)
            gk = Gemm(KLH, KLL, None)
            gp = Gemm(ULH, ULL, None)
            go = Gemm(BH, BL, None)
            T = {}
            cgl = lambda name, n: col[name][:, n * l:n * l + n]

            def start():
                t = stt(SCL[:, :], MOD[:, l, 16:32], 1.0, cgl("norm_g_2", 16), ALU.add, ALU.mult, mod_tok[l], C["vc"], scl.get("r"))
                SC.wait(t, C["vc"])
                C["scl"] = t
                yield from xprep(gz, SCL, MOD[:, l, 0:16], gz_free[l]())
                T["pad"] = VE.do(lambda e: e.memset(UT[:, :, 0:30], 0.0), rms["n"])
                for tab, gi in ((TQ, 2 * l), (TK, 2 * l + 1)):
                    for i, (gs, f) in enumerate(((0, 0), (32, 1), (32, 0), (0, 1))):
                        T["tab"] = tt(PO, tab[:, i, :, :], CS[:, f, :, :],
                                      TRG[:, gi:gi + 1, gs:gs + 32].to_broadcast([128, 2, 32]), ALU.mult, C["cs"], v_tok)
                spawn(after_conv())

            uv = {}
            conv = {}

            def z_done(c, p, tok):
                pp = [P[:, 2 * p, :], P[:, 2 * p + 1, :]]
                if c in (0, 2):
                    for t in range(2):
                        te = copy_act(UV[:, t, :], pp[t], tok, T.get("uvr"))
                    pairs.release(p, te)
                    T["uv"] = te
                    return
                if c in (1, 3):
                    j = c // 2
                    for t in range(2):
                        te = copy_act(UG[:, t, :], pp[t], tok, T.get("uvr"))
                    pairs.release(p, te)
                    bg = cgl("glu_b_2", 16)
                    yield
                    for i in range(4):
                        ct = 4 * j + i
                        b, pb, wb = bank()
                        for t in range(2):
                            tr(pb[:, t * 128:(t + 1) * 128], UV[:, t, i * 128:(i + 1) * 128], IDN, wb, te, T["uv"])
                            last = tr(pb[:, 256 + t * 128:256 + (t + 1) * 128], UG[:, t, i * 128:(i + 1) * 128], IDN, inc=(t == 1))
                        fs, wf = f_slots.take()
                        ta = act(FB[:, fs, 0:256], pb[:, 256:512], ACT.Sigmoid, last, wf, bias=bg[:, 8 + ct:9 + ct])
                        tb = stt(UT[:, ct, 30:286], pb[:, 0:256], bg[:, ct:ct + 1], FB[:, fs, 0:256], ALU.add, ALU.mult, ta, T["pad"])
                        f_slots.release(fs, tb)
                        t_slots.release(b, tb)
                        conv[ct] = tb
                        if i % 2:
                            yield
                    T["uvr"] = last
                    spawn(convolve(range(4 * j, 4 * j + 4), (3, 6, 7)))
                    return
                if c == 4:
                    for t in range(2):
                        te = copy_act(NQ[:, t, :], pp[t], tok)
                    pairs.release(p, te)
                    yield from latent(NQ, 512, te, 6, gq, QLH, QLL, cgl("q_lat_g_2", 4))
                    return
                if c == 5:
                    for t in range(2):
                        te = copy_act(NK[:, t, :], pp[t][:, 0:256], tok)
                        te = copy_act(KR[:, t, :], pp[t][:, 256:320], tok)
                    pairs.release(p, te)
                    q = tt(PO, FBk, KR[:, :, :], KR[:, :, :], ALU.mult, te)
                    T["ssr"] = red(ST[:, 56:58], FBk, ALU.add, q)
                    q = te
                    T["rk"] = rope(RK[:, :, :], KR[:, :, :], TK, 1, q)
                    yield from latent(NK, 256, te, 14, gk, KLH, KLL, cgl("kv_lat_g_2", 2))
                    return
                dst = SMG if c < 8 else SCG
                o = (c % 2) * 512
                for t in range(2):
                    te = act(dst[:, t, o:o + 512], pp[t], ACT.Silu if c < 8 else ACT.Copy, tok)
                pairs.release(p, te)
                T["g", c] = te

            FBk = UTk[:, :].rearrange("p (a b) -> p a b", a=2)

            def rope(o, x, tab, n, *w):
                tb = [tab[:, i, :, :].rearrange("p t (h f) -> p t h f", h=1).to_broadcast([128, 2, n, 32]) for i in range(4)]
                tm = [RT[:, i * 128:i * 128 + n * 64].rearrange("p (t h f) -> p t h f", t=2, h=n) for i in range(2)]
                o4, x4 = (v.rearrange("p (t h) f -> p t h f", t=2) for v in (o, x))
                x1, x2, o1, o2_ = x4[:, :, :, 0:32], x4[:, :, :, 32:64], o4[:, :, :, 0:32], o4[:, :, :, 32:64]
                tt(PO, o1, x1, tb[0], ALU.mult, T["tab"], *w)
                q0 = tt(PO, tm[0], x2, tb[1], ALU.mult)
                tt(PO, o2_, x2, tb[2], ALU.mult)
                q1 = tt(PO, tm[1], x1, tb[3], ALU.mult)
                tt(PO, o1, o1, tm[0], ALU.subtract, q0)
                return tt(PO, o2_, o2_, tm[1], ALU.add, q1)

            def latent(NAT, n, te, o, g, H, L, gain):
                for t in range(2):
                    fs, wf = f_slots.take()
                    q = act(FB[:, fs, 0:n], NAT[:, t, :], ACT.Square, te, wf, accum_out=ST[:, o + t:o + t + 1])
                    f_slots.release(fs, q)
                q = ts(VE, ST[:, o + 2:o + 4], ST[:, o:o + 2], 1.0 / n, EPS, ALU.mult, ALU.add, q)
                q = power(ST[:, o + 4:o + 6], ST[:, o + 2:o + 4], 2, q)
                for _ in range(4 if n == 512 else 3):
                    yield
                for t in range(2):
                    q2 = ts(VE, NAT[:, t, :], NAT[:, t, :], ST[:, o + 4 + t:o + 5 + t], None, ALU.mult, None, q)
                yield
                yield
                yield from flips(lambda kt, t: NAT[:, t, kt * 128:(kt + 1) * 128], range(0, n // 128, 2), lambda k: q2, g.tok,
                                 H, L, lambda n: affine(gain, None, SC))

            def convolve(cts, pool):
                while cts[0] and "conv0" not in T:
                    yield
                ctok = {}
                for k in range(31):
                    for ct in cts:
                        x, w, cb = UT[:, ct, k:k + 256], DW[:, l, ct, k:k + 1], cgl("dw_b_2", 8)[:, ct:ct + 1]
                        if ct in pool and k == 0:
                            ctok[ct] = act(CA[:, ct, :], x, ACT.Identity, conv[ct], C["dw"], scale=w, bias=cb)
                        elif ct in pool:
                            s, wp = p_slots.take()
                            ta = act(PB[:, s, :], x, ACT.Copy, conv[ct], C["dw"], wp, scale=w)
                            ctok[ct] = tt(PO, CA[:, ct, :], CA[:, ct, :], PB[:, s, :], ALU.add, ta, ctok[ct])
                            p_slots.release(s, ctok[ct])
                        elif k == 0:
                            ctok[ct] = ts(VE, CA[:, ct, :], x, w, cb, ALU.mult, ALU.add, conv[ct], C["dw"])
                        else:
                            ctok[ct] = stt(CA[:, ct, :], x, w, CA[:, ct, :], ALU.mult, ALU.add, ctok[ct])
                    if k % 4 < 3:
                        yield
                T["conv0" if cts[0] == 0 else "conv1"] = list(ctok.values())
                if cts[0]:
                    T["conv"] = T["conv0"] + T["conv1"]

            def layernorm():
                b, pb, wb = bank()
                for ct in range(8):
                    last = mm(pb[:, 0:256], ONE, CA[:, ct, :], ct == 0, ct == 7, wb, T["conv"], inc=(ct == 7))
                mu = LNS[:, 0, :]
                t = ts(VE, mu, pb[:, 0:256], 1.0 / 1024, None, ALU.mult, None, last)
                t_slots.release(b, t)
                for i in range(2):
                    ca = CA[:, 4 * i:4 * i + 4, :]
                    t = tt(VE, ca, ca, LNS[:, 0:1, :].to_broadcast([128, 4, 256]), ALU.subtract, t)
                    yield
                yield
                yield
                b, pb, wb = bank()
                for cp in range(4):
                    fs, wf = f_slots.take()
                    q = act(FB[:, fs, :], CA[:, 2 * cp:2 * cp + 2, :].rearrange("p a b -> p (a b)"), ACT.Square, t, wf)
                    for i in range(2):
                        for tk in range(2):
                            last = mm(pb[:, tk:tk + 1], FB[:, fs, i * 256 + tk * 128:i * 256 + (tk + 1) * 128], ONE[:, 0:1],
                                      cp == 0 and i == 0 and tk == 0, cp == 3 and i == 1 and tk == 1, wb, q,
                                      inc=(i == 1 and tk == 1), skip_group_check=True)
                    f_slots.release(fs, last)
                q = ts(VE, ST[:, 76:78], pb[:, 0:2], 1.0 / 1024, EPS, ALU.mult, ALU.add, last)
                t_slots.release(b, q)
                q = power(ST[:, 78:80], ST[:, 76:78], 2, q)
                yield
                b, pb, wb = bank()
                for t in range(2):
                    last = mm(pb[:, t * 128:(t + 1) * 128], ST[:, 78 + t:79 + t].to_broadcast([128, 128]), IDN, True, True, wb, q, inc=(t == 1))
                q = copy_dve(LNS[:, 2, :], pb[:, 0:256], last)
                t_slots.release(b, q)
                q = tt(VE, CA[:, :, :], CA[:, :, :], LNS[:, 2:3, :].to_broadcast([128, 8, 256]), ALU.mult, q)
                while "zend" not in T:
                    yield
                SC.wait(gz.end)
                SC.ops.append(lambda e: e.dma_start(BR[0:1, :], A["b_pw_2"][l:l + 1, :]).then_inc(s_br, 16))
                lg, lb = cgl("conv_ln_g_2", 8), cgl("conv_ln_b_2", 8)
                for cp in range(4):
                    fs, wf = f_slots.take()
                    for i in range(2):
                        ct = 2 * cp + i
                        te = act(FB[:, fs, i * 256:(i + 1) * 256], CA[:, ct, :], ACT.Silu, q, wf, scale=lg[:, ct:ct + 1], bias=lb[:, ct:ct + 1])
                    tl = split(FB[:, fs, :], fs, te, ULH[:, 2 * cp:2 * cp + 2, :].rearrange("p a b -> p (a b)"),
                               ULL[:, 2 * cp:2 * cp + 2, :].rearrange("p a b -> p (a b)"), gz.end)
                    gp.tok[2 * cp] = gp.tok[2 * cp + 1] = tl
                    yield
                g = SCG[:, :, :].rearrange("p t n -> p (t n)")
                T["silu"] = act(g, g, ACT.Silu, T["g", 9])

            att = dict(q=[], k=[], free_nat=None, freeT=None, freeKV=None)

            def q_done(g, p, tok):
                while att.get("busyq"):
                    yield
                att["busyq"] = True
                fs, wf = f_slots.take()
                copy_act(QN[:, 0, :], P[:, 2 * p, 0:384], tok, att.get("rq"))
                te = copy_act(QN[:, 1, :], P[:, 2 * p + 1, 0:384])
                pairs.release(p, te)
                for t in range(2):
                    for h in range(2):
                        q = act(FB[:, fs, h * 192:(h + 1) * 192], QN[:, t, h * 192:(h + 1) * 192], ACT.Square, wf, te if t == 0 else q, accum_out=ST[:, 20 + 2 * t + h:21 + 2 * t + h])
                f_slots.release(fs, q)
                q = ts(VE, ST[:, 24:28], ST[:, 20:24], 1.0 / 192, EPS, ALU.mult, ALU.add, q)
                q = power(ST[:, 28:32], ST[:, 24:28], 4, q)
                x = QN[:, :, :].rearrange("p t (h d) -> p (t h) d", h=2)
                q = tt(PO, x, x, ST[:, 28:32].rearrange("p (a b) -> p a b", b=1).to_broadcast([128, 4, 192]), ALU.mult, q)
                yield
                att["qn"] = rope(QR[:, :, :], x[:, :, 128:192], TQ, 2, q, att.get("rq"))

            def kv_done(g, p, tok):
                while att.get("busyk"):
                    yield
                att["busyk"] = True
                for t in range(2):
                    te = copy_act(KV[:, t, :], P[:, 2 * p + t, :], tok, att.get("rkv"))
                pairs.release(p, te)
                kv = KV[:, :, :].rearrange("p t (h d) -> p (t h) d", h=2)
                kn = kv[:, :, 0:128]
                fs, wf = f_slots.take()
                for t in range(2):
                    for h in range(2):
                        q = act(FB[:, fs, (2 * t + h) * 128:(2 * t + h + 1) * 128], KV[:, t, h * 256:h * 256 + 128], ACT.Square, wf, te, accum_out=ST[:, 32 + 2 * t + h:33 + 2 * t + h])
                f_slots.release(fs, q)
                for t in range(2):
                    q2 = ts(VE, ST[:, 36 + 2 * t:38 + 2 * t], ST[:, 32 + 2 * t:34 + 2 * t], ST[:, 56 + t:57 + t], 1.0 / 192, ALU.add, ALU.mult, q, T["ssr"])
                q = ts(VE, ST[:, 36:40], ST[:, 36:40], EPS, None, ALU.add, None, q2)
                q = power(ST[:, 40:44], ST[:, 36:40], 4, q)
                q1 = tt(PO, kn, kn, ST[:, 40:44].rearrange("p (a b) -> p a b", b=1).to_broadcast([128, 4, 128]), ALU.mult, q)
                q1 = tt(PO, KR2[:, :, :].rearrange("p (t h) d -> p t h d", t=2),
                        RK[:, :, :].rearrange("p t (h d) -> p t h d", h=1).to_broadcast([128, 2, 2, 64]),
                        ST[:, 40:44].rearrange("p (t h d) -> p t h d", t=2, d=1).to_broadcast([128, 2, 2, 64]), ALU.mult, q, T["rk"],
                        att.get("rkr"))
                yield
                while "qn" not in att:
                    yield
                qn = att.pop("qn")
                yield
                yield
                yield
                tt_tok = []
                for which in range(4):
                    b, pb, wb = bank()
                    rows = 128 if which < 2 else 64
                    for h in range(2):
                        for t in range(2):
                            o = pb[0:rows, (2 * h + t) * 128:(2 * h + t + 1) * 128]
                            src = (QN[:, t, h * 192:h * 192 + 128], KV[:, t, h * 256:h * 256 + 128], QR[:, 2 * t + h, :], KR2[:, 2 * t + h, :])[which]
                            last = tr(o, src, IDN, wb, qn, q1, inc=(h == 1 and t == 1))
                    if which == 0:
                        te = ts(VE, TT[0:rows, which, :], pb[0:rows, :], GQ[:, 1 + l:2 + l], None, ALU.mult, None, last, att.get("rT"))
                    else:
                        te = copy_act(TT[0:rows, which, :], pb[0:rows, :], last, att.get("rT"))
                    tt_tok.append(te)
                    t_slots.release(b, te)
                    if which == 1:
                        yield
                att["rq"] = att["rkr"] = last
                att["busyq"] = False
                yield
                isc = 192.0 ** -0.5
                ex = []
                for h in range(2):
                    b, pb, wb = bank()
                    for t, (o, n) in enumerate(((0, 128), (128, 256))):
                        qs, ks = slice(h * 256 + t * 128, h * 256 + t * 128 + 128), slice(h * 256, h * 256 + n)
                        mm(pb[:, o:o + n], TT[:, 0, qs], TT[:, 1, ks], True, False, wb, tt_tok)
                        last = mm(pb[:, o:o + n], TT[0:64, 2, qs], TT[0:64, 3, ks], False, True, inc=(t == 1))
                    dg = SCO[:, h, :].rearrange("p (a b) -> p a b", b=128)[:, 0:3:2, :]
                    pd = pb[:, 0:384].rearrange("p (a b) -> p a b", b=128)[:, 0:3:2, :]
                    ta = tt(VE, dg, pd, NM.rearrange("p (a b) -> p a b", a=1).to_broadcast([128, 2, 128]), ALU.add, last, att.get("rS"))
                    tb = copy_dve(SCO[:, h, 128:256], pb[:, 128:256], last, att.get("rS"))
                    t_slots.release(b, tb)
                    m = ST[:, 44 + 2 * h:46 + 2 * h]
                    red(m[:, 0:1], SCO[:, h, 0:128], ALU.max, ta, tb)
                    tm = red(m[:, 1:2], SCO[:, h, 128:384], ALU.max, ta, tb)
                    tm = ts(VE, m, m, -isc, None, ALU.mult, None, tm)
                    act(SCO[:, h, 0:128], SCO[:, h, 0:128], ACT.Exp, tm, scale=isc, bias=m[:, 0:1], accum_out=ST[:, 48 + 2 * h:49 + 2 * h])
                    te = act(SCO[:, h, 128:384], SCO[:, h, 128:384], ACT.Exp, scale=isc, bias=m[:, 1:2], accum_out=ST[:, 49 + 2 * h:50 + 2 * h])
                    ex.append(te)
                ri = VE.do(lambda e: e.reciprocal(ST[:, 52:56], ST[:, 48:52]), ex)
                att["rT"] = last
                yield
                yield
                pt = []
                for h in range(2):
                    b, pb, wb = bank()
                    for i in range(3):
                        last = tr(pb[:, i * 128:(i + 1) * 128], SCO[:, h, i * 128:(i + 1) * 128], IDN, wb, ex[h], inc=(i == 2))
                    te = copy_act(PTB[:, h, :], pb[:, 0:384], last, att.get("rP"))
                    t_slots.release(b, te)
                    pt.append(te)
                att["rS"] = last
                yield
                while ("g", 6 + g // 2) not in T:
                    yield
                b, pb, wb = bank()
                for h in range(2):
                    v0, v1 = (KV[:, t, h * 256 + 128:h * 256 + 256] for t in range(2))
                    o0, o1 = (pb[:, (2 * t + h) * 128:(2 * t + h + 1) * 128] for t in range(2))
                    mm(o0, PTB[:, h, 0:128], v0, True, True, wb, pt)
                    mm(o1, PTB[:, h, 128:256], v0, True, False)
                    last = mm(o1, PTB[:, h, 256:384], v1, False, True, inc=(h == 1))
                att["rkv"] = att["rP"] = last
                fs, wf = f_slots.take()
                f = FB[:, fs, :]
                for t in range(2):
                    for h in range(2):
                        s = slice((2 * t + h) * 128, (2 * t + h + 1) * 128)
                        te = stt(f[:, s], pb[:, s], ST[:, 52 + 2 * h + t:53 + 2 * h + t], SMG[:, t, (2 * g + h) * 128:(2 * g + h + 1) * 128],
                                 ALU.mult, ALU.mult, last, wf, ri, T["g", 6 + g // 2])
                t_slots.release(b, te)
                yield
                flast, tl = flip(lambda kt, t: f[:, (2 * t + kt - 2 * g) * 128:(2 * t + kt - 2 * g + 1) * 128], (2 * g, 2 * g + 1), te, go.tok,
                                 BH[:, 2 * g:2 * g + 2, :].rearrange("p a b -> p (a b)"), BL[:, 2 * g:2 * g + 2, :].rearrange("p a b -> p (a b)"),
                                 plain)
                f_slots.release(fs, flast)
                att["busyk"] = False

            def z_end():
                T["zend"] = True

            def after_conv():
                while "conv" not in T:
                    yield
                yield from layernorm()
                for j in range(4):
                    b, pb, wb = bank()
                    for i in range(4):
                        gc = MOD[:, l, 32 + 4 * j + i:33 + 4 * j + i].to_broadcast([128, 128])
                        last = mm(pb[:, i * 128:(i + 1) * 128], gc, IDN, True, True, wb, inc=(i == 3))
                    T["G", j] = copy_act(G[:, j * 512:(j + 1) * 512], pb, last)
                    t_slots.release(b, T["G", j])
                    yield

            def p_done(c, p, tok):
                while "silu" not in T:
                    yield
                for t in range(2):
                    te = tt(VE, MP[:, t, :], P[:, 2 * p + t, :], SCG[:, t, c * 512:(c + 1) * 512], ALU.mult, tok, T["silu"], T.get("mp"))
                pairs.release(p, te)
                yield
                for last, _ in flips(lambda kt, t: MP[:, t, (kt - 8 - 4 * c) * 128:(kt - 7 - 4 * c) * 128], (8 + 4 * c, 10 + 4 * c), lambda k: te,
                                     go.tok, BH, BL, lambda n: plain):
                    T["mp"] = last
                    yield

            def o_done(c, p, tok):
                for t in range(2):
                    fs, wf = f_slots.take()
                    te = tt(VE, FB[:, fs, :], P[:, 2 * p + t, :], G[:, c * 512:(c + 1) * 512], ALU.mult, tok, T["G", c], wf)
                    o = X[:, t, c * 512:(c + 1) * 512]
                    xs[(c, t)] = tx = tt(VE if c == 3 else PO, o, o, FB[:, fs, :], ALU.add, te, xs[(c, t)], rms["n"])
                    f_slots.release(fs, tx)
                pairs.release(p, te)
                if l == 0:
                    x_square(c)
                if l == 1:
                    for t in range(2):
                        SP.wait(xs[(c, t)])
                        SP.ops.append(lambda e, t=t: e.dma_start(out[0, t * 128:(t + 1) * 128, c * 512:(c + 1) * 512],
                                                                 X[:, t, c * 512:(c + 1) * 512]).then_inc(s_out, 16))
                return
                yield

            def bias(o, c):
                mm(o, ONE[0:1, :], BR[0:1, c * 512:(c + 1) * 512], True, False, (s_br, 16 * (l + 1)))

            gz.done, gq.done, gk.done, gp.done, go.done = z_done, q_done, kv_done, p_done, o_done
            gp.bias = bias
            w_in, w_o = A["w_in_2"][l], A["w_out_2"][l]
            zc = [(1856, 512), (2880, 512), (2368, 512), (3392, 512), (0, 512), (512, 320), (832, 512), (1344, 512), (3904, 512), (4416, 512)]

            def z_units(c):
                c0, w = zc[c]
                for k in range(0, 16, 2):
                    unit(gz, c, w_in, k * 128, k, 2, c0, w, k == 0, k == 14)

            def up_units(g):
                for k in (0, 2):
                    unit(gq, g, A["w_q_up_2"][l], k * 128, k, 2, 384 * g, 384, k == 0, k == 2)
                unit(gk, g, A["w_kv_up_2"][l], 0, 0, 2, 512 * g, 512, True, True)

            for c in range(7):
                z_units(c)
            for g in range(3):
                up_units(g)
                z_units(7 + g)
            gz.last_unit = plan[-1]
            gz.fence = z_end
            up_units(3)

            def p_units(c):
                for k in range(0, 8, 2):
                    unit(gp, c, A["w_pw_2"][l], k * 128, k, 2, 512 * c, 512, k == 0, k == 6)

            def o_units(c, ks):
                for k in ks:
                    unit(go, c, w_o, k * 128, k, 2, 512 * c, 512, k == 0, k == 14)

            o_units(0, (0, 2))
            p_units(0)
            o_units(0, (4,))
            p_units(1)
            o_units(0, (6, 8, 10))
            o_units(1, (0, 2))
            o_units(0, (12, 14))
            o_units(1, range(4, 16, 2))
            for c in (2, 3):
                o_units(c, range(0, 16, 2))
            go.last_unit = plan[-1]
            return start, go

        s_out = sem("s_out")
        scl = {}
        gz_free = {}
        UTk = put("UTk", [128, 128], off=oBL + 6 * K)
        RT = put("RT", [128, 256], off=oBL + 6 * K + 512)

        wq, wo = A["sb_w_qkv"][0], A["sb_w_o"][0]
        for j in range(4):
            for kind in range(3):
                for k in range(0, 16, 2):
                    unit(g_qkv, 3 * j + kind, wq, k * 128, k, 2, kind * 2048 + 512 * j, 512, k == 0, k == 14)
        for cs in ((0, 1), (2, 3)):
            for lo, hi in ((0, 12), (12, 16)):
                for c in cs:
                    for k in range(lo, hi, 2):
                        unit(g_wo, c, wo, k * 128, k, 2, 512 * c, 512, k == 0, k == 14)

        def m1_units(e):
            for c in range(2):
                for k in range(0, 16, 2):
                    unit(g_m1, 2 * e + c, A["mlp_w_in"][0], k * 128, k, 2, (2 * e + c) * 512, 512, k == 0, k == 14)

        def m2_units(e):
            for c in range(4):
                for k in range(0, 8, 2):
                    unit(m2[e], c, A["mlp_w_out"][0], e * 1024 + k * 128, k, 2, 512 * c, 512, k == 0, k == 6)

        m1_units(0)
        for e in range(1, 8):
            m1_units(e)
            m2_units(e - 1)
        m2_units(7)
        first_end = len(plan)
        m2[7].last_unit = plan[-1]
        start0, go0 = layer(0)
        start1, go1 = layer(1)
        gz_free[0] = lambda: g_m1.end
        gz_free[1] = lambda: go0.end

        def begin(start):
            spawn(start())
            pump()

        m2[7].fence = lambda: begin(start0)
        go0.fence = lambda: begin(start1)

        adas = [(l, pc, kt) for l in range(2) for pc in range(6) for kt in range(16)]
        for i, u in enumerate(plan):
            items.append(("w", u))
            while adas and i >= 16 and 192 - len(adas) < 192 * (i - 15) / (first_end - 48):
                items.append(("a", adas.pop(0)))
        for c in range(4):
            load_x(c)
            issue_dma()
        issue_dma()
        for dst, src, k in vload:
            SP.ops.append(lambda e, dst=dst, src=src, k=k: e.dma_start(dst, src, **k).then_inc(s_v, 16))
        spawn(x_start())
        spawn(load_vectors())
        pump()
        run()
        SP.ops.append(lambda e: e.wait_ge(s_out, 128))

        block = ctx.enter_context(nc.Block())

        @block.sync
        def _(e):
            for f in SP.ops:
                f(e)

        @block.scalar
        def _(e):
            for f in SC.ops:
                f(e)

        @block.vector
        def _(e):
            for f in VE.ops:
                f(e)

        @block.gpsimd
        def _(e):
            for f in PO.ops:
                f(e)

        @block.tensor
        def _(e):
            for f in PE.ops:
                f(e)


def constants():
    c = np.zeros((128, 6 * 128 + 33), np.float32)
    p, f = np.arange(128)[:, None], np.arange(128)[None, :]
    c[:, 0:128] = p == f
    c[:, 128:256] = p < f
    c[:, 256:384] = -(p > f).astype(np.float32)
    c[:, 384:512] = -1.0
    c[:, 512:640] = np.where(f <= p, 0.0, -1e30)
    c[:, 640:768] = 1.0
    e = np.arange(0, 64, 2, dtype=np.float32) / np.float32(64)
    c[:, 768:800] = np.float32(1.0) / np.power(np.float32(10000.0), e)
    c[:, 800] = -0.5
    return c


_INS = ["x", "norm_mix_g", "norm_mlp_g", "sb_w_qkv", "sb_q_norm_g", "sb_k_norm_g", "sb_w_o", "mlp_w_in", "mlp_w_out",
        "c_2", "positions_2", "ada_w_2", "ada_b_2", "norm_g_2", "w_in_2", "q_lat_g_2", "w_q_up_2", "kv_lat_g_2",
        "w_kv_up_2", "q_norm_g_2", "k_norm_g_2", "glu_b_2", "dw_w_2", "dw_b_2", "conv_ln_g_2", "conv_ln_b_2",
        "w_pw_2", "b_pw_2", "w_out_2"]


def kernel(**inputs):
    import concourse.bacc as _bacc
    from concourse.bass_utils import run_bass_kernel_spmd as _run

    nc = _bacc.Bacc("TRN2", target_bir_lowering=False, num_devices=1)
    arrays, args = {}, {}
    given = {name: np.ascontiguousarray(inputs[name]) for name in _INS}
    given["consts"] = constants()
    for name, a in given.items():
        arrays[f"in_{name}_dram"] = a
        args[name] = nc.dram_tensor(f"in_{name}_dram", a.shape, mybir.dt.from_np(a.dtype), kind="ExternalInput").ap()
    out = nc.dram_tensor("out_0_dram", (1, 256, 2048), F32, kind="ExternalOutput").ap()
    build(nc, args, out)
    r = _run(nc, [arrays], core_ids=[0])
    return r.results[0]["out_0_dram"]
```
